# Optimizing a Trainium2 kernel written in Bass

```python
import math
import jax, jax.numpy as jnp
from jax import lax
import numpy as np

D_MODEL = 1024
BATCH = 1
SEQ = 256
DEPTH = 1

MIX_WIDTH = D_MODEL
HEAD_DIM = 64
A_WIDTH = D_MODEL // 4
B_WIDTH = D_MODEL // 2
C_WIDTH = D_MODEL // 4
A_HEADS = A_WIDTH // HEAD_DIM
B_HEADS = B_WIDTH // HEAD_DIM
C_GROUPS = C_WIDTH // HEAD_DIM
IN_COLS = 2 * A_WIDTH + 3 * B_WIDTH + 2 * C_WIDTH
CHUNK = 128
MOBA_BLOCK = 256
MOBA_TOPK = 3
Q_BLK = 64
CONV_WIDTH = 31
MEM_LEN = 256
X_HEADS = 4
X_HEAD_DIM = D_MODEL // X_HEADS
D_FF = 4 * D_MODEL
EPS = 1e-6


def rms_norm(x, g):
    xf = x.astype(jnp.float32)
    y = xf * lax.rsqrt(jnp.mean(xf * xf, axis=-1, keepdims=True) + EPS)
    return (y * g.astype(jnp.float32)).astype(x.dtype)

def layer_norm(x, g, b):
    xf = x.astype(jnp.float32)
    mu = jnp.mean(xf, axis=-1, keepdims=True)
    xc = xf - mu
    var = jnp.mean(xc * xc, axis=-1, keepdims=True)
    y = xc * lax.rsqrt(var + EPS) * g.astype(jnp.float32) + b.astype(jnp.float32)
    return y.astype(x.dtype)

def alibi_slopes(n_heads):
    return 2.0 ** (-8.0 * jnp.arange(1, n_heads + 1, dtype=jnp.float32) / n_heads)

def spatial_gating(z, ln_g, ln_b, w_s, b_s):
    Bn, S, _ = z.shape
    u, v = jnp.split(z, 2, axis=-1)
    v = layer_norm(v, ln_g, ln_b)
    v = v.reshape(Bn, S // CHUNK, CHUNK, A_HEADS, HEAD_DIM)
    causal = jnp.tril(jnp.ones((CHUNK, CHUNK), dtype=w_s.dtype))
    w = (w_s * causal[None]).astype(v.dtype)
    mixed = jnp.einsum('hts,bcshd->bcthd', w, v) + b_s.T.astype(v.dtype)[None, None, :, :, None]
    return u * mixed.reshape(Bn, S, A_WIDTH)

def moba_attention(q, k, v):
    Bn, H, S, Dh = q.shape
    s_pad = -(-S // MOBA_BLOCK) * MOBA_BLOCK
    pad = ((0, 0), (0, 0), (0, s_pad - S), (0, 0))
    q, k, v = jnp.pad(q, pad), jnp.pad(k, pad), jnp.pad(v, pad)
    nb = s_pad // MOBA_BLOCK
    kk = min(MOBA_TOPK, nb)
    n_q = s_pad // Q_BLK
    scale = Dh ** -0.5
    slopes = alibi_slopes(H)
    kb = k.reshape(Bn, H, nb, MOBA_BLOCK, Dh)
    vb = v.reshape(Bn, H, nb, MOBA_BLOCK, Dh)
    kmean = jnp.mean(kb.astype(jnp.float32), axis=3)
    qc = q.reshape(Bn, H, n_q, Q_BLK, Dh).transpose(2, 0, 1, 3, 4)
    bi = jnp.arange(Bn)[:, None, None, None]
    hi = jnp.arange(H)[None, :, None, None]
    offs = jnp.arange(MOBA_BLOCK)

    def one_block(args):
        qi, ci = args
        t = ci * Q_BLK + jnp.arange(Q_BLK)
        own = (ci * Q_BLK) // MOBA_BLOCK
        gate = jnp.einsum('bhqd,bhnd->bhqn', qi.astype(jnp.float32), kmean)
        gate = jnp.where(jnp.arange(nb) < own, gate, -jnp.inf)
        _, idx = lax.top_k(gate, kk)
        valid = idx < own
        ksel = kb[bi, hi, idx]
        vsel = vb[bi, hi, idx]
        s_past = jnp.einsum('bhqd,bhqkld->bhqkl', qi, ksel).astype(jnp.float32) * scale
        kpos = idx[..., None] * MOBA_BLOCK + offs
        dist = (t[None, None, :, None, None] - kpos).astype(jnp.float32)
        s_past = jnp.where(valid[..., None], s_past - slopes[None, :, None, None, None] * dist, -jnp.inf)
        k_own = lax.dynamic_index_in_dim(kb, own, axis=2, keepdims=False)
        v_own = lax.dynamic_index_in_dim(vb, own, axis=2, keepdims=False)
        s_own = jnp.einsum('bhqd,bhld->bhql', qi, k_own).astype(jnp.float32) * scale
        kpos_own = own * MOBA_BLOCK + offs
        dist_own = (t[:, None] - kpos_own[None, :]).astype(jnp.float32)
        s_own = jnp.where((dist_own >= 0)[None, None],
                          s_own - slopes[None, :, None, None] * dist_own[None, None], -jnp.inf)
        s_all = jnp.concatenate([s_past.reshape(Bn, H, Q_BLK, kk * MOBA_BLOCK), s_own], axis=-1)
        p = jax.nn.softmax(s_all, axis=-1).astype(v.dtype)
        p_past = p[..., :kk * MOBA_BLOCK].reshape(Bn, H, Q_BLK, kk, MOBA_BLOCK)
        p_own = p[..., kk * MOBA_BLOCK:]
        return (jnp.einsum('bhqkl,bhqkld->bhqd', p_past, vsel)
                + jnp.einsum('bhql,bhld->bhqd', p_own, v_own))

    out = lax.map(one_block, (qc, jnp.arange(n_q, dtype=jnp.int32)))
    out = out.transpose(1, 0, 3, 2, 4).reshape(Bn, s_pad, H * Dh)
    return out[:, :S]

def conformer_conv(z, w_dw, b_dw, gn_g, gn_b):
    Bn, S, _ = z.shape
    a, g = jnp.split(z, 2, axis=-1)
    y = a * jax.nn.sigmoid(g)
    rhs = w_dw.astype(y.dtype)[:, None, :]
    y = lax.conv_general_dilated(y, rhs, window_strides=(1,), padding=[(CONV_WIDTH - 1, 0)],
                                 dimension_numbers=('NWC', 'WIO', 'NWC'),
                                 feature_group_count=C_WIDTH)
    y = y + b_dw.astype(y.dtype)
    y = y.reshape(Bn, S, C_GROUPS, HEAD_DIM)
    y = layer_norm(y, gn_g.reshape(C_GROUPS, HEAD_DIM), gn_b.reshape(C_GROUPS, HEAD_DIM))
    return jax.nn.silu(y.reshape(Bn, S, C_WIDTH))

def memory_cross_attention(h, m, w_q, w_kv, w_o):
    Bn, S, _ = h.shape
    M = m.shape[1]
    q = (h @ w_q).reshape(Bn, S, X_HEADS, X_HEAD_DIM)
    k, v = jnp.split(m @ w_kv, 2, axis=-1)
    k = k.reshape(Bn, M, X_HEADS, X_HEAD_DIM)
    v = v.reshape(Bn, M, X_HEADS, X_HEAD_DIM)
    s = jnp.einsum('bshd,bmhd->bhsm', q, k).astype(jnp.float32) * (X_HEAD_DIM ** -0.5)
    p = jax.nn.softmax(s, axis=-1).astype(v.dtype)
    o = jnp.einsum('bhsm,bmhd->bshd', p, v).reshape(Bn, S, D_MODEL)
    return o @ w_o

def first_inputs(seed: int = 0) -> dict:
    key = jax.random.key(seed)
    ks = jax.random.split(key, 24)
    f32 = jnp.float32
    L = DEPTH

    def nrm(k, shape, scale):
        return jax.random.normal(k, shape, f32) * scale

    def gain(k, shape):
        return 1.0 + 0.05 * jax.random.normal(k, shape, f32)

    return {
        "x": nrm(ks[0], (BATCH, SEQ, D_MODEL), 1.0),
        "mem": nrm(ks[1], (BATCH, MEM_LEN, D_MODEL), 1.0),
        "pre_mix_g": gain(ks[2], (L, D_MODEL)),
        "w_in": nrm(ks[3], (L, D_MODEL, IN_COLS), D_MODEL ** -0.5),
        "gate_ln_g": gain(ks[4], (L, A_WIDTH)),
        "gate_ln_b": nrm(ks[5], (L, A_WIDTH), 0.02),
        "w_s": nrm(ks[6], (L, A_HEADS, CHUNK, CHUNK), CHUNK ** -0.5),
        "b_s": nrm(ks[7], (L, A_HEADS, CHUNK), 0.02),
        "w_dw": nrm(ks[8], (L, CONV_WIDTH, C_WIDTH), CONV_WIDTH ** -0.5),
        "b_dw": nrm(ks[9], (L, C_WIDTH), 0.02),
        "conv_gn_g": gain(ks[10], (L, C_WIDTH)),
        "conv_gn_b": nrm(ks[11], (L, C_WIDTH), 0.02),
        "w_out": nrm(ks[12], (L, MIX_WIDTH, D_MODEL), MIX_WIDTH ** -0.5),
        "post_mix_g": gain(ks[13], (L, D_MODEL)),
        "pre_x_g": gain(ks[14], (L, D_MODEL)),
        "mem_g": gain(ks[15], (L, D_MODEL)),
        "w_xq": nrm(ks[16], (L, D_MODEL, D_MODEL), D_MODEL ** -0.5),
        "w_xkv": nrm(ks[17], (L, D_MODEL, 2 * D_MODEL), D_MODEL ** -0.5),
        "w_xo": nrm(ks[18], (L, D_MODEL, D_MODEL), D_MODEL ** -0.5),
        "post_x_g": gain(ks[19], (L, D_MODEL)),
        "pre_ffn_g": gain(ks[20], (L, D_MODEL)),
        "w_ff1": nrm(ks[21], (L, D_MODEL, D_FF), D_MODEL ** -0.5),
        "w_ff2": nrm(ks[22], (L, D_FF, D_MODEL), D_FF ** -0.5),
        "post_ffn_g": gain(ks[23], (L, D_MODEL)),
    }

def first_block(x, mem, pre_mix_g, w_in, gate_ln_g, gate_ln_b, w_s, b_s, w_dw, b_dw,
              conv_gn_g, conv_gn_b, w_out, post_mix_g, pre_x_g, mem_g, w_xq, w_xkv,
              w_xo, post_x_g, pre_ffn_g, w_ff1, w_ff2, post_ffn_g):
    Bn, S, _ = x.shape
    split_a = 2 * A_WIDTH
    split_b = split_a + 3 * B_WIDTH
    for l in range(DEPTH):
        h = rms_norm(x, pre_mix_g[l])
        z = h @ w_in[l]
        za, zb, zc = z[..., :split_a], z[..., split_a:split_b], z[..., split_b:]
        ya = spatial_gating(jax.nn.gelu(za, approximate=False),
                            gate_ln_g[l], gate_ln_b[l], w_s[l], b_s[l])
        q, k, v = jnp.split(zb, 3, axis=-1)
        q, k, v = (a.reshape(Bn, S, B_HEADS, HEAD_DIM).transpose(0, 2, 1, 3) for a in (q, k, v))
        yb = moba_attention(q, k, v)
        yc = conformer_conv(zc, w_dw[l], b_dw[l], conv_gn_g[l], conv_gn_b[l])
        y = jnp.concatenate([ya, yb, yc], axis=-1) @ w_out[l]
        x = x + rms_norm(y, post_mix_g[l])
        h = rms_norm(x, pre_x_g[l])
        m = rms_norm(mem, mem_g[l])
        x = x + rms_norm(memory_cross_attention(h, m, w_xq[l], w_xkv[l], w_xo[l]), post_x_g[l])
        h = rms_norm(x, pre_ffn_g[l])
        f = jnp.square(jax.nn.relu(h @ w_ff1[l])) @ w_ff2[l]
        x = x + rms_norm(f, post_ffn_g[l])
    return x


DEPTH_2 = 2

N_MIXERS = 3
GRID_W = 64
Q_BLOCK = 128
D_FF_2 = 2816
FFN_RES = 0.5

DIFF_HEAD_DIM = 64
DIFF_HEADS = D_MODEL // (2 * DIFF_HEAD_DIM)
ROPE_THETA = 500000.0
ROPE_DIMS = DIFF_HEAD_DIM // 4

NA_HEAD_DIM = 64
NA_HEADS = D_MODEL // NA_HEAD_DIM
NA_WIN_H = 8
NA_WIN_W = 16

GQA_HEAD_DIM = 64
GQA_Q_HEADS = D_MODEL // GQA_HEAD_DIM
GQA_KV_HEADS = GQA_Q_HEADS // 4
AXIAL_THETA = 10000.0

N_A = len(range(0, DEPTH_2, N_MIXERS))
N_B = len(range(1, DEPTH_2, N_MIXERS))
N_C = len(range(2, DEPTH_2, N_MIXERS))


def _rmsnorm(x, g):
    xf = x.astype(jnp.float32)
    y = xf * lax.rsqrt(jnp.mean(xf * xf, axis=-1, keepdims=True) + EPS)
    return (y * g.astype(jnp.float32)).astype(x.dtype)

def _swiglu(x, wg, wu, wd):
    return (jax.nn.silu(x @ wg) * (x @ wu)) @ wd

def _rope_angles(pos, dims, theta):
    inv = theta ** (-jnp.arange(0, dims, 2, dtype=jnp.float32) / dims)
    return pos[:, None] * inv[None, :]

def _rotate(x, ang):
    m = ang.shape[1]
    ang = ang.reshape((1, ang.shape[0]) + (1,) * (x.ndim - 3) + (m,))
    cos = jnp.cos(ang).astype(x.dtype)
    sin = jnp.sin(ang).astype(x.dtype)
    x1, x2 = x[..., :m], x[..., m:]
    return jnp.concatenate([x1 * cos - x2 * sin, x2 * cos + x1 * sin], axis=-1)

def _to_blocks(q):
    b, s = q.shape[:2]
    return jnp.moveaxis(q.reshape((b, s // Q_BLOCK, Q_BLOCK) + q.shape[2:]), 1, 0)

def _from_blocks(o):
    o = jnp.moveaxis(o, 0, 1)
    return o.reshape((o.shape[0], o.shape[1] * o.shape[2]) + o.shape[3:])

def _diff_attention(h, w_in, w_out, lam_vecs, subln_g, layer_idx):
    b, s, _ = h.shape
    nh, dh = DIFF_HEADS, DIFF_HEAD_DIM
    q, k, v = jnp.split(h @ w_in, 3, axis=-1)
    q = q.reshape(b, s, nh, 2, dh)
    k = k.reshape(b, s, nh, 2, dh)
    v = v.reshape(b, s, nh, 2 * dh)
    ang = _rope_angles(jnp.arange(s, dtype=jnp.float32), ROPE_DIMS, ROPE_THETA)
    q = jnp.concatenate([_rotate(q[..., :ROPE_DIMS], ang), q[..., ROPE_DIMS:]], axis=-1)
    k = jnp.concatenate([_rotate(k[..., :ROPE_DIMS], ang), k[..., ROPE_DIMS:]], axis=-1)
    lam_init = 0.8 - 0.6 * math.exp(-0.3 * layer_idx)
    lv = lam_vecs.astype(jnp.float32)
    lam = jnp.exp(jnp.sum(lv[0] * lv[1])) - jnp.exp(jnp.sum(lv[2] * lv[3])) + lam_init
    scale = dh ** -0.5

    def block(qb):
        sc = jnp.einsum('bqhcd,bshcd->bhcqs', qb, k).astype(jnp.float32) * scale
        p = jax.nn.softmax(sc, axis=-1)
        a = (p[:, :, 0] - lam * p[:, :, 1]).astype(v.dtype)
        return jnp.einsum('bhqs,bshe->bqhe', a, v)

    o = _from_blocks(lax.map(block, _to_blocks(q)))
    o = _rmsnorm(o, subln_g) * (1.0 - lam_init)
    return o.reshape(b, s, nh * 2 * dh) @ w_out

def _neighborhood_attention(h, w_in, w_out, rpb):
    b, s, _ = h.shape
    nh, dh = NA_HEADS, NA_HEAD_DIM
    rows = s // GRID_W
    kh = min(NA_WIN_H, rows)
    kw = NA_WIN_W
    q, k, v = jnp.split(h @ w_in, 3, axis=-1)
    q = q.reshape(b, rows, GRID_W, nh, dh)
    k = k.reshape(b, rows, GRID_W, nh, dh)
    v = v.reshape(b, rows, GRID_W, nh, dh)
    cols = jnp.arange(GRID_W)
    col_start = jnp.clip(cols - kw // 2, 0, GRID_W - kw)
    col_idx = col_start[:, None] + jnp.arange(kw)[None, :]
    dc = col_idx - cols[:, None] + (NA_WIN_W - 1)
    scale = dh ** -0.5

    def row_step(r):
        r0 = jnp.clip(r - kh // 2, 0, rows - kh)
        dr = r0 + jnp.arange(kh) - r + (NA_WIN_H - 1)
        k_band = lax.dynamic_slice_in_dim(k, r0, kh, axis=1)
        v_band = lax.dynamic_slice_in_dim(v, r0, kh, axis=1)
        k_win = k_band[:, :, col_idx]
        v_win = v_band[:, :, col_idx]
        q_row = lax.dynamic_index_in_dim(q, r, axis=1, keepdims=False)
        bias = rpb[:, dr[None, :, None], dc[:, None, :]]
        sc = jnp.einsum('bqhd,brqjhd->bhqrj', q_row, k_win).astype(jnp.float32) * scale
        sc = sc + bias.astype(jnp.float32)[None]
        p = jax.nn.softmax(sc.reshape(b, nh, GRID_W, kh * kw), axis=-1)
        p = p.reshape(sc.shape).astype(v.dtype)
        return jnp.einsum('bhqrj,brqjhd->bqhd', p, v_win)

    o = lax.map(row_step, jnp.arange(rows))
    o = jnp.moveaxis(o, 0, 1).reshape(b, s, nh * dh)
    return o @ w_out

def _gqa_axial(h, w_in, w_out, qk_g):
    b, s, _ = h.shape
    nq, nkv, dh = GQA_Q_HEADS, GQA_KV_HEADS, GQA_HEAD_DIM
    grp = nq // nkv
    qkv = h @ w_in
    q = qkv[..., :nq * dh].reshape(b, s, nkv, grp, dh)
    k = qkv[..., nq * dh:(nq + nkv) * dh].reshape(b, s, nkv, dh)
    v = qkv[..., (nq + nkv) * dh:].reshape(b, s, nkv, dh)
    q = _rmsnorm(q, qk_g[0])
    k = _rmsnorm(k, qk_g[1])
    t = jnp.arange(s)
    half = dh // 2
    ang_r = _rope_angles((t // GRID_W).astype(jnp.float32), half, AXIAL_THETA)
    ang_c = _rope_angles((t % GRID_W).astype(jnp.float32), half, AXIAL_THETA)
    q = jnp.concatenate([_rotate(q[..., :half], ang_r), _rotate(q[..., half:], ang_c)], axis=-1)
    k = jnp.concatenate([_rotate(k[..., :half], ang_r), _rotate(k[..., half:], ang_c)], axis=-1)
    scale = dh ** -0.5

    def block(qb):
        sc = jnp.einsum('bqkgd,bskd->bkgqs', qb, k).astype(jnp.float32) * scale
        p = jax.nn.softmax(sc, axis=-1).astype(v.dtype)
        return jnp.einsum('bkgqs,bskd->bqkgd', p, v)

    o = _from_blocks(lax.map(block, _to_blocks(q)))
    return o.reshape(b, s, nq * dh) @ w_out

def second_inputs(seed: int = 0) -> dict:
    key = jax.random.key(seed)
    ks = jax.random.split(key, 20)

    def w(k, shape, fan_in):
        return jax.random.normal(k, shape, jnp.float32) * fan_in ** -0.5

    def gain(k, shape):
        return 1.0 + 0.05 * jax.random.normal(k, shape, jnp.float32)

    diff_w = DIFF_HEADS * 2 * DIFF_HEAD_DIM
    na_w = NA_HEADS * NA_HEAD_DIM
    gqa_q = GQA_Q_HEADS * GQA_HEAD_DIM
    gqa_in = (GQA_Q_HEADS + 2 * GQA_KV_HEADS) * GQA_HEAD_DIM
    return {
        'x': jax.random.normal(ks[0], (BATCH, SEQ, D_MODEL), jnp.float32),
        'norm_g': gain(ks[1], (DEPTH_2, 6, D_MODEL)),
        'ffn1_wg': w(ks[2], (DEPTH_2, D_MODEL, D_FF_2), D_MODEL),
        'ffn1_wu': w(ks[3], (DEPTH_2, D_MODEL, D_FF_2), D_MODEL),
        'ffn1_wd': w(ks[4], (DEPTH_2, D_FF_2, D_MODEL), D_FF_2),
        'ffn2_wg': w(ks[5], (DEPTH_2, D_MODEL, D_FF_2), D_MODEL),
        'ffn2_wu': w(ks[6], (DEPTH_2, D_MODEL, D_FF_2), D_MODEL),
        'ffn2_wd': w(ks[7], (DEPTH_2, D_FF_2, D_MODEL), D_FF_2),
        'diff_w_in': w(ks[8], (N_A, D_MODEL, 3 * diff_w), D_MODEL),
        'diff_w_out': w(ks[9], (N_A, diff_w, D_MODEL), diff_w),
        'diff_lambda': 0.1 * jax.random.normal(ks[10], (N_A, 4, DIFF_HEAD_DIM), jnp.float32),
        'diff_subln': gain(ks[11], (N_A, 2 * DIFF_HEAD_DIM)),
        'na_w_in': w(ks[12], (N_B, D_MODEL, 3 * na_w), D_MODEL),
        'na_w_out': w(ks[13], (N_B, na_w, D_MODEL), na_w),
        'na_rpb': 0.1 * jax.random.normal(ks[14], (N_B, NA_HEADS, 2 * NA_WIN_H - 1, 2 * NA_WIN_W - 1), jnp.float32),
        'gqa_w_in': w(ks[15], (N_C, D_MODEL, gqa_in), D_MODEL),
        'gqa_w_out': w(ks[16], (N_C, gqa_q, D_MODEL), gqa_q),
        'gqa_qk_norm': gain(ks[17], (N_C, 2, GQA_HEAD_DIM)),
    }

def second_block(x, norm_g, ffn1_wg, ffn1_wu, ffn1_wd, ffn2_wg, ffn2_wu, ffn2_wd,
              diff_w_in, diff_w_out, diff_lambda, diff_subln,
              na_w_in, na_w_out, na_rpb,
              gqa_w_in, gqa_w_out, gqa_qk_norm):
    h = x
    for i in range(DEPTH_2):
        g = norm_g[i]
        h = h + FFN_RES * _rmsnorm(_swiglu(_rmsnorm(h, g[0]), ffn1_wg[i], ffn1_wu[i], ffn1_wd[i]), g[1])
        u = _rmsnorm(h, g[2])
        kind, j = i % N_MIXERS, i // N_MIXERS
        if kind == 0:
            m = _diff_attention(u, diff_w_in[j], diff_w_out[j], diff_lambda[j], diff_subln[j], i)
        elif kind == 1:
            m = _neighborhood_attention(u, na_w_in[j], na_w_out[j], na_rpb[j])
        else:
            m = _gqa_axial(u, gqa_w_in[j], gqa_w_out[j], gqa_qk_norm[j])
        h = h + _rmsnorm(m, g[3])
        h = h + FFN_RES * _rmsnorm(_swiglu(_rmsnorm(h, g[4]), ffn2_wg[i], ffn2_wu[i], ffn2_wd[i]), g[5])
    return h


def setup_inputs(seed=0):
    out = dict(first_inputs(seed))
    for name, value in second_inputs(seed + 1).items():
        if name != "x":
            out[name + "_2"] = value
    return out


def reference(
    x, mem, pre_mix_g, w_in, gate_ln_g, gate_ln_b, w_s, b_s, w_dw, b_dw, conv_gn_g, conv_gn_b,
    w_out, post_mix_g, pre_x_g, mem_g, w_xq, w_xkv, w_xo, post_x_g, pre_ffn_g, w_ff1, w_ff2,
    post_ffn_g, norm_g_2, ffn1_wg_2, ffn1_wu_2, ffn1_wd_2, ffn2_wg_2, ffn2_wu_2, ffn2_wd_2,
    diff_w_in_2, diff_w_out_2, diff_lambda_2, diff_subln_2, na_w_in_2, na_w_out_2, na_rpb_2,
    gqa_w_in_2, gqa_w_out_2, gqa_qk_norm_2,
):
    x = first_block(
        x, mem, pre_mix_g, w_in, gate_ln_g, gate_ln_b, w_s, b_s, w_dw, b_dw, conv_gn_g,
        conv_gn_b, w_out, post_mix_g, pre_x_g, mem_g, w_xq, w_xkv, w_xo, post_x_g, pre_ffn_g,
        w_ff1, w_ff2, post_ffn_g,
    )
    return second_block(
        x, norm_g_2, ffn1_wg_2, ffn1_wu_2, ffn1_wd_2, ffn2_wg_2, ffn2_wu_2, ffn2_wd_2,
        diff_w_in_2, diff_w_out_2, diff_lambda_2, diff_subln_2, na_w_in_2, na_w_out_2, na_rpb_2,
        gqa_w_in_2, gqa_w_out_2, gqa_qk_norm_2,
    )


_drawn_inputs = setup_inputs


def setup_inputs(seed=0):
    import zlib

    import numpy as np

    out = dict(_drawn_inputs(seed))
    spreads = {}
    factors = {'gate_ln_g': 10.465,
     'gate_ln_b': 21.841,
     'b_s': 16.519,
     'conv_gn_b': 12.221,
     'na_rpb_2': 5.675,
     'b_dw': 3.172,
     'conv_gn_g': 2.922,
     'diff_lambda_2': 2.835}
    for name, (base, spread) in spreads.items():
        noise = np.random.default_rng([zlib.crc32(name.encode()), seed]).standard_normal(out[name].shape)
        drawn = base * np.exp(spread * noise) if base else spread * noise
        out[name] = __import__('jax').numpy.asarray(drawn.astype(out[name].dtype))
    for name, factor in factors.items():
        out[name] = (out[name] * factor).astype(out[name].dtype)
    return out
```

```python
from contextlib import ExitStack

import numpy as np

import concourse.bass as bass
from concourse import mybir

F32 = mybir.dt.float32
F32R = mybir.dt.float32r
ACT = mybir.ActivationFunctionType
ALU = mybir.AluOpType
AX_X = mybir.AxisListType.X

P = 128
D = 1024
S = 256
KT = D // P
TT = S // P
EPS = 1e-6
NSLOT = 3
CH = 2048
FF1, FF2 = 4096, 2816
RELU_BLOCKS = FF1 // 256
GLU_BLOCKS = FF2 // 256
FAR = 1e30

C_MEMK = 0
C_MEMV = C_MEMK + 4
C_WIN = C_MEMV + 4
C_WOUT = C_WIN + 10
C_XQ = C_WOUT + 4
C_XO = C_XQ + 4
C_RELU = C_XO + 4
C_LAYER = C_RELU + 2 * RELU_BLOCKS
PER_LAYER = 2 * 3 * GLU_BLOCKS + 16
N_CHUNKS = C_LAYER + 2 * PER_LAYER


def c_layer(layer):
    c = C_LAYER + layer * PER_LAYER
    return c, c + 3 * GLU_BLOCKS, c + 3 * GLU_BLOCKS + 12, c + 3 * GLU_BLOCKS + 16


ATT = {
    "moba": dict(units=8, u0=0, e0=0, heads_per_out=2, scale=0.125, parts=1),
    "cross": dict(units=4, u0=8, e0=4, heads_per_out=1, scale=1.0 / 16, parts=1),
    "diff": dict(units=8, u0=12, e0=8, heads_per_out=1, scale=0.125, parts=2),
    "near": dict(units=16, u0=20, e0=16, heads_per_out=2, scale=0.125, parts=1),
}
LAM_INIT = 0.8 - 0.6 * float(np.exp(-0.3 * 0))


def shape_tables():
    t = np.arange(S)
    q = np.arange(P)
    dist = np.zeros((P, TT, S), np.float32)
    for tt in range(TT):
        d = (tt * P + q)[:, None] - t[None, :]
        dist[:, tt] = np.where(d >= 0, d, FAR)
    ident = np.eye(P, dtype=np.float32)
    group = np.kron(np.eye(2), np.ones((64, 64))).astype(np.float32) / np.float32(64)
    mean = np.full((P, P), 1 / P, np.float32)
    rot = np.zeros((P, P), np.float32)
    inv = np.float32(500000.0) ** (-np.arange(0, 16, 2, dtype=np.float32) / np.float32(16))
    ang = (t.astype(np.float32)[:, None] * inv[None, :].astype(np.float32)).astype(np.float32)
    cos = np.ones((P, S), np.float32)
    sin = np.zeros((P, S), np.float32)
    for base in (0, 64):
        for j in range(8):
            rot[base + j + 8, base + j] = -1.0
            rot[base + j, base + j + 8] = 1.0
            for o in (0, 8):
                cos[base + j + o] = np.cos(ang[:, j])
                sin[base + j + o] = np.sin(ang[:, j])
    col = np.arange(64)
    start = np.clip(col - 8, 0, 48)
    inside = (col[None, :] >= start[:, None]) & (col[None, :] < start[:, None] + 16)
    window = np.tile(np.where(inside, 0.0, -FAR).astype(np.float32), (2, 1))
    return np.concatenate([ident, group, mean, rot, cos, sin, window, dist.reshape(P, -1)], axis=1)


TABLE_COLS = 4 * P + 2 * S + 64


def build(nc, w, table, out):
    with ExitStack() as ctx:
        def sb(name, shape, dt=F32):
            return ctx.enter_context(nc.sbuf_tensor(name, shape, dt))

        def sem(name):
            return ctx.enter_context(nc.semaphore(name))

        raw = sb("raw", [P, NSLOT, CH])
        w_hi = sb("w_hi", [P, NSLOT, CH], F32R)
        w_lo = sb("w_lo", [P, NSLOT, CH], F32R)
        x = sb("x_rows", [P, TT, D])
        t1 = sb("t1", [P, TT, D])
        hT = (sb("hT_hi", [P, KT, S], F32R), sb("hT_lo", [P, KT, S], F32R))
        yT = (sb("yT_hi", [P, KT, S], F32R), sb("yT_lo", [P, KT, S], F32R))
        hid = (sb("hid_hi", [P, 2, S], F32R), sb("hid_lo", [P, 2, S], F32R))
        qT = sb("qT", [P, KT, S])
        kT = sb("kT", [P, KT, S])
        vv = sb("vv", [P, TT, D])
        big = sb("big", [P, 3 * CH])
        kmT = big[:, 0:CH].rearrange("p (k s) -> p k s", k=KT)
        vm = big[:, CH:2 * CH].rearrange("p (t d) -> p t d", t=TT)
        uT = big[:, 2 * CH:2 * CH + 512]
        va = big[:, 2 * CH + 512:2 * CH + 1024].rearrange("p (t d) -> p t d", t=TT)
        sig = big[:, 2 * CH + 1024:2 * CH + 1536]
        glu_a = big[:, 2 * CH + 1536:3 * CH]
        bias = big[:, :].rearrange("p (h j c) -> p h j c", h=16, j=6)
        conv_in = qT[:, 4:7, :].rearrange("p a b -> p (a b)")[:, 0:2 * 286].rearrange("p (i t) -> p i t", i=2)
        b_mix = kT[:, 4:6, :]
        ln_g = kT[:, 6, :]
        ln_b = kT[:, 7, :]
        wsT = vv[:, 0, 512:1024].rearrange("p (h t) -> p h t", h=4)
        dist = vv[:, 1, 512:1024]
        gain = sb("gain", [P, 2, D])
        att_bias = sb("att_bias", [P, 2, 512])
        prob = sb("prob", [P, 2, 512])
        probT = sb("probT", [P, 2, 512])
        expd = t1[:, :, :]
        ws_raw = att_bias[:, 0, :].rearrange("p (h t) -> p h t", h=4)
        tab = sb("tab", [P, TABLE_COLS])
        ident = tab[:, 0:P]
        group_mean = tab[:, P:2 * P]
        all_mean = tab[:, 2 * P:3 * P]
        rot = tab[:, 3 * P:4 * P]
        cos = tab[:, 4 * P:4 * P + S]
        sin = tab[:, 4 * P + S:4 * P + 2 * S]
        window = tab[:, 4 * P + 2 * S:TABLE_COLS]
        par_rows = sb("par_rows", [69, P])
        par = sb("par", [P, 70])
        lam_rows = sb("lam_rows", [P, 4, 64])
        lam = sb("lam", [P, 8])
        minus_half = sb("minus_half", [P, S])
        ssq = sb("ssq", [P, 64])
        rstd = sb("rstd", [P, 64])
        top = sb("top", [P, 2, 4])
        neg_top = sb("neg_top", [P, 2, 4])
        denom = sb("denom", [P, 2, 4])
        inv_denom = sb("inv_denom", [P, 2, 4])
        ln_s = sb("ln_s", [P, 8])
        hraw = t1[:, 0, 0:512]
        gate = t1[:, 0, 512:1024]
        rope_t = t1[:, 1, 0:512]
        sub_sq = att_bias
        sub_out = sb("sub_out", [P, 2, S])

        ps = ctx.enter_context(nc.psum_tensor("ps", [P, 8, 512], F32))

        landed = [sem(f"chunk_landed_{s}") for s in range(NSLOT)]
        hi_done, lo_done, used = sem("hi_done"), sem("lo_done"), sem("chunk_used")
        gains_in = [sem("gain_post_in"), sem("gain_pre_in")]
        x_in, mem_in, tab_in, small_in = sem("x_in"), sem("mem_in"), sem("tab_in"), sem("small_in")
        bias_in, out_done = sem("bias_in"), sem("out_done")
        masked, const_set = sem("ws_masked"), sem("const_set")
        par_T, par_ready = sem("par_transposed"), sem("par_ready")
        y_half, sq_post, r_post, t1_post, x_new = (sem(n) for n in ("y_half", "sq_post", "r_post", "t1_post", "x_new"))
        sq_pre, r_pre, normed, turned, h_hi, h_lo = (sem(n) for n in ("sq_pre", "r_pre", "normed", "turned", "h_hi", "h_lo"))
        b_evac, v_evac = sem("b_evac"), sem("v_evac")
        gate_done, hraw_done, hid_hi, hid_lo = (sem(n) for n in ("gate_done", "hraw_done", "hid_hi_done", "hid_lo_done"))
        s_ready, m_ready, e_ready, p_ready, t_ready, pt_ready, o_ready, o_hi, o_lo = (
            sem(n) for n in ("scores_ready", "max_ready", "exp_ready", "prob_ready", "probT_turned", "probT_ready",
                             "out_ready", "out_hi", "out_lo"))
        rot_ready, rope_mul, rope_done = sem("rot_ready"), sem("rope_mul"), sem("rope_done")
        sub_sq_done, sub_ms, sub_var, sub_r, sub_on = (sem(n) for n in ("sub_sq", "sub_ms", "sub_var", "sub_r", "sub_on"))
        v_centered, v_sq, v_r, v_normed, mix_ready, ya_raw, glu_ready, conv_done = (
            sem(n) for n in ("v_centered", "v_sq", "v_r", "v_normed", "mix_ready", "ya_raw", "glu_ready", "conv_done"))
        cm_ready, c_centered, c_sq, c_var, c_eps, c_r, c_norm, c_silu, yc_hi, yc_lo, ya_hi, ya_lo = (
            sem(n) for n in ("conv_mean", "conv_centered", "conv_sq", "conv_var", "conv_eps", "conv_r", "conv_norm",
                             "conv_silu", "yc_hi", "yc_lo", "ya_hi", "ya_lo"))
        lam_dot, lam_exp, lam_ready, bias_masked = sem("lam_dot"), sem("lam_exp"), sem("lam_ready"), sem("bias_masked")
        dve_link, act_link, pool_link = sem("dve_link"), sem("act_link"), sem("pool_link")

        def linker(eng, link_sem):
            count = [0]

            def link(ins):
                count[0] += 1
                ins.then_inc(link_sem, 1)
                eng.wait_ge(link_sem, count[0])
            return link

        def row_bcast(ap, n):
            return bass.AP(ap.tensor, ap.offset, [[0, P], [1, n]])

        def b_bank(n):
            return ps[:, 4 + n % 2, :]

        B_MEMK, B_WIN, B_XQ, B_DIFF, B_NEAR = 0, 4, 12, 16, 24
        NORM_LAST = [C_WOUT + 3, C_XO + 3, C_LAYER - 1]
        for layer in range(2):
            f1, cin, cout, f2 = c_layer(layer)
            NORM_LAST += [cin - 1, cout + 3, f2 + 3 * GLU_BLOCKS - 1]
        N_NORMS = len(NORM_LAST)
        half = {2: 0.5, 3: 0.5, 5: 0.5, 6: 0.5, 8: 0.5}
        half.pop(2)
        post_gains = [w["post_mix_g"][0], w["post_x_g"][0], w["post_ffn_g"][0]] + [
            w["norm_g_2"][layer, j] for layer in range(2) for j in (1, 3, 5)]
        pre_gains = [w["mem_g"][0], w["pre_mix_g"][0], w["pre_x_g"][0], w["pre_ffn_g"][0]] + [
            w["norm_g_2"][layer, j] for layer in range(2) for j in (0, 2, 4)]

        def wcols(m, c0, n, k0=0, kn=KT):
            return m[k0 * P:(k0 + kn) * P, c0:c0 + n].rearrange("(k p) n -> p k n", p=P)

        block = ctx.enter_context(nc.Block())

        @block.sync
        def _(sp):
            def load(c, src, dims=KT):
                slot = c % NSLOT if isinstance(c, int) else None
                if c >= NSLOT:
                    sp.wait_ge(lo_done, c - NSLOT + 1)
                sp.dma_start(raw[:, slot, :].rearrange("p (k n) -> p k n", k=dims), src).then_inc(landed[slot], 16)

            def load_in_loop(c0, i, per, j, src, dims=KT):
                slot = (c0 + j) % NSLOT
                sp.wait_ge(lo_done, i * per + (c0 + j - NSLOT + 1))
                sp.dma_start(raw[:, slot, :].rearrange("p (k n) -> p k n", k=dims), src).then_inc(landed[slot], 16)

            def load_pre_gain(n):
                if n:
                    sp.wait_ge(normed, TT * n)
                sp.dma_start(gain[:, 1, :], row_bcast(pre_gains[n], D)).then_inc(gains_in[1], 16)

            def load_gains(j):
                if j:
                    sp.wait_ge(t1_post, TT * j)
                sp.dma_start(gain[:, 0, :], row_bcast(post_gains[j], D)).then_inc(gains_in[0], 16)
                if j < N_NORMS - 1:
                    load_pre_gain(2 + j)

            def transposed(c0, m, col, n):
                for j in range(n):
                    load(c0 + j, wcols(m, col + 256 * j, 256))

            def rows(c0, m, col, n):
                for j in range(n):
                    load(c0 + j, wcols(m, col + 512 * (j // 2), 512, 4 * (j % 2), 4), 4)

            def load_bias(p0, n):
                sp.wait_ge(o_lo, ATT["diff"]["e0"])
                rpb = w["na_rpb_2"]
                for p in range(p0, p0 + n):
                    r, c = p // 64, p % 64
                    sp.dma_start(bias[p:p + 1], bass.AP(rpb.tensor, (5 - r) * 31 + 15 - c, [[465, 16], [31, 6], [1, 64]])
                                 ).then_inc(bias_in, 16)

            sp.dma_start(t1[:, :, :], w["mem"][0].rearrange("(t p) d -> p t d", p=P)).then_inc(mem_in, 16)
            load_pre_gain(0)
            sp.dma_start(tab[:, :], table[:, 0:TABLE_COLS]).then_inc(tab_in, 16)
            sp.dma_start(x[:, :, :], w["x"][0].rearrange("(t p) d -> p t d", p=P)).then_inc(x_in, 16)
            w_xkv, w_in = w["w_xkv"][0], w["w_in"][0]
            transposed(C_MEMK, w_xkv, 0, 3)
            load_pre_gain(1)
            load(C_MEMK + 3, wcols(w_xkv, 768, 256))
            rows(C_MEMV, w_xkv, D, 4)
            for j, col in enumerate((2304, 2048, 0, 256, 512, 768, 1024, 1280)):
                load(C_WIN + j, wcols(w_in, col, 256))
            rows(C_WIN + 8, w_in, 1536, 2)
            rows(C_WOUT, w["w_out"][0], 0, 4)
            load_gains(0)
            transposed(C_XQ, w["w_xq"][0], 0, 4)
            rows(C_XO, w["w_xo"][0], 0, 4)
            load_gains(1)

            up, down = w["w_ff1"][0], w["w_ff2"][0]
            load(C_RELU, wcols(up, 0, 256))
            with sp.Fori(0, (RELU_BLOCKS - 1) // 3) as i:
                for j in range(3):
                    load_in_loop(C_RELU + 1, i, 6, 2 * j,
                                 up[:, bass.ds(i * 768 + (256 * j + 256), 256)].rearrange("(k p) n -> p k n", p=P))
                    load_in_loop(C_RELU + 1, i, 6, 2 * j + 1,
                                 down[bass.ds(i * 768 + 256 * j, 256), :].rearrange("(k p) n -> p k n", p=P), 2)
            load(C_LAYER - 1, down[FF1 - 256:FF1, :].rearrange("(k p) n -> p k n", p=P), 2)
            load_gains(2)

            def gated(c0, which, layer, j):
                wg, wu, wd = (w[f"{which}_{n}_2"][layer] for n in ("wg", "wu", "wd"))
                load(c0, wcols(wg, 0, 256))
                load(c0 + 1, wcols(wu, 0, 256))
                with sp.Fori(0, GLU_BLOCKS - 1) as i:
                    load_in_loop(c0 + 2, i, 3, 0, wg[:, bass.ds(i * 256 + 256, 256)].rearrange("(k p) n -> p k n", p=P))
                    load_in_loop(c0 + 2, i, 3, 1, wu[:, bass.ds(i * 256 + 256, 256)].rearrange("(k p) n -> p k n", p=P))
                    load_in_loop(c0 + 2, i, 3, 2, wd[bass.ds(i * 256, 256), :].rearrange("(k p) n -> p k n", p=P), 2)
                load(c0 + 3 * GLU_BLOCKS - 1, wd[FF2 - 256:FF2, :].rearrange("(k p) n -> p k n", p=P), 2)
                load_gains(j)

            for layer, (m_in, m_out) in enumerate((("diff_w_in_2", "diff_w_out_2"), ("na_w_in_2", "na_w_out_2"))):
                f1, cin, cout, f2 = c_layer(layer)
                gated(f1, "ffn1", layer, 3 + 3 * layer)
                for j in range(8):
                    load(cin + j, wcols(w[m_in][0], 256 * j, 256))
                    if layer == 0:
                        load_bias(16 * j, 16)
                rows(cin + 8, w[m_in][0], 2048, 4)
                rows(cout, w[m_out][0], 0, 4)
                load_gains(4 + 3 * layer)
                gated(f2, "ffn2", layer, 5 + 3 * layer)
            for t in range(TT):
                sp.wait_ge(x_new, TT * (N_NORMS - 1) + t + 1)
                sp.dma_start(out[0, t * P:(t + 1) * P, :], x[:, t, :]).then_inc(out_done, 16)
            sp.wait_ge(out_done, 16 * TT)

        @block.gpsimd
        def _(pool):
            link = linker(pool, pool_link)
            pool.memset(minus_half[:, :], -0.5).then_inc(const_set, 1)
            pool.memset(conv_in[:, :, 0:30], 0.0).then_inc(const_set, 1)
            n = 0
            for dst, src in (
                (ws_raw, w["w_s"][0].rearrange("h t s -> t h s")),
                (par_rows[0:62, :], w["w_dw"][0].rearrange("k (i p) -> (k i) p", p=P)),
                (par_rows[62:64, :], w["b_dw"][0].rearrange("(i p) -> i p", p=P)),
                (par_rows[64:66, :], w["conv_gn_g"][0].rearrange("(i p) -> i p", p=P)),
                (par_rows[66:68, :], w["conv_gn_b"][0].rearrange("(i p) -> i p", p=P)),
                (par_rows[68:69, :], w["diff_subln_2"][0:1, :]),
                (ln_g, row_bcast(w["gate_ln_g"][0], 256)),
                (ln_b, row_bcast(w["gate_ln_b"][0], 256)),
                (lam_rows[:, :, :].rearrange("p a b -> p (a b)"), row_bcast(w["diff_lambda_2"][0, 0], 256)),
                (dist, table[:, TABLE_COLS:TABLE_COLS + 512]),
            ):
                pool.dma_start(dst, src).then_inc(small_in, 16)
                n += 1
            bs = w["b_s"][0]
            for h in range(4):
                for c in range(TT):
                    pool.dma_start(b_mix[64 * (h % 2):64 * (h % 2) + 64, h // 2, c * P:(c + 1) * P],
                                   bass.AP(bs.tensor, bs.offset + h * P, [[0, 64], [1, P]])).then_inc(small_in, 16)
                    n += 1
            assert n == 18
            pool.wait_ge(small_in, 16 * 18)
            pool.affine_select(out=ws_raw, in_=ws_raw, compare_op=ALU.is_ge, fill=0.0, base=0,
                               pattern=[[0, 4], [-1, P]], channel_multiplier=1).then_inc(masked, 1)

            def inverse_root(dst, src, ready, count, done):
                pool.wait_ge(ready, count)
                link(pool.tensor_scalar(dst, src, EPS, None, ALU.add))
                pool.tensor_tensor(dst, dst, minus_half[:, 0:1], ALU.pow).then_inc(done, 1)

            def pre_norm(n):
                for t in range(TT):
                    k = TT * n + t
                    inverse_root(rstd[:, k:k + 1], ssq[:, k:k + 1], sq_pre, k + 1, r_pre)

            def norm(j):
                for t in range(TT):
                    k = 32 + TT * j + t
                    inverse_root(rstd[:, k:k + 1], ssq[:, k:k + 1], sq_post, TT * j + t + 1, r_post)
                if j < N_NORMS - 1:
                    pre_norm(2 + j)

            pool.wait_ge(const_set, 1)
            pre_norm(0)
            pre_norm(1)
            for t in range(TT):
                inverse_root(ln_s[:, 6 + t:7 + t], ln_s[:, 4 + t:5 + t], v_sq, t + 1, v_r)
            for i in range(2):
                pool.wait_ge(c_eps, 1)
                v = glu_a[:, 256 * i:256 * i + 256]
                pool.tensor_tensor(v, v, minus_half[:, :], ALU.pow).then_inc(c_r, 1)
            norm(0)
            norm(1)
            norm(2)
            norm(3)
            for u in range(8):
                pool.wait_ge(sub_var, u + 1)
                if u >= 2:
                    pool.wait_ge(sub_on, u - 1)
                pool.tensor_tensor(sub_sq[:, u % 2, 256:512], sub_sq[:, u % 2, 256:512], minus_half[:, :],
                                   ALU.pow).then_inc(sub_r, 1)
            norm(4)
            pool.wait_ge(bias_in, 16 * P)
            for h in range(16):
                pool.tensor_tensor(bias[:, h], bias[:, h],
                                   window.rearrange("p (j c) -> p j c", j=1).broadcast_to([P, 6, 64]),
                                   ALU.add).then_inc(bias_masked, 1)
            for j in range(5, N_NORMS):
                norm(j)

        @block.scalar
        def _(act):
            link = linker(act, act_link)

            def split(c):
                if c >= N_CHUNKS:
                    return
                slot = c % NSLOT
                act.wait_ge(landed[slot], 16 * (c // NSLOT + 1))
                if c >= NSLOT:
                    act.wait_ge(used, c - NSLOT + 1)
                act.copy(w_hi[:, slot, :], raw[:, slot, :]).then_inc(hi_done, 1)

            def split_in_loop(c, i, per):
                if isinstance(i, int):
                    return split(c + i * per)
                slot = c % NSLOT
                act.wait_ge(landed[slot], i * (16 * per // NSLOT) + 16 * (c // NSLOT + 1))
                act.wait_ge(used, i * per + (c - NSLOT + 1))
                act.copy(w_hi[:, slot, :], raw[:, slot, :]).then_inc(hi_done, 1)

            def squares(n, src_ready):
                src = t1 if n == 0 else x
                for t in range(TT):
                    src_ready(t)
                    k = TT * n + t
                    act.activation(ps[:, 2 * t:2 * t + 2, :].rearrange("p a b -> p (a b)"), src[:, t, :], ACT.Square,
                                   scale=1.0 / 32, accum_out=ssq[:, k:k + 1]).then_inc(sq_pre, 1)

            def turned_hi(n, dst):
                for b in range(4):
                    t, k0 = b // 2, 4 * (b % 2)
                    act.wait_ge(turned, 4 * n + b + 1)
                    act.copy(dst[0][:, k0:k0 + 4, t * P:(t + 1) * P],
                             ps[:, 4 + b, :].rearrange("p (k s) -> p k s", k=4)).then_inc(h_hi, 1)

            def norm(j):
                for t in range(TT):
                    if t == 0:
                        act.wait_ge(y_half, j + 1)
                    else:
                        act.wait_ge(used, NORM_LAST[j] + 1)
                    k = 32 + TT * j + t
                    act.activation(t1[:, t, :], ps[:, 2 * t:2 * t + 2, :].rearrange("p a b -> p (a b)"), ACT.Square,
                                   scale=1.0 / 32, accum_out=ssq[:, k:k + 1]).then_inc(sq_post, 1)
                if j < N_NORMS - 1:
                    squares(2 + j, lambda t: act.wait_ge(x_new, TT * j + t + 1))
                    turned_hi(2 + j, hT)

            def evac_b(n, c, dst):
                act.wait_ge(used, c + 1)
                act.copy(dst, b_bank(n).rearrange("p (a s) -> p a s", a=2)).then_inc(b_evac, 1)
                split(c + NSLOT)

            def evac_v(c0, n, dst):
                for c in range(c0, c0 + n):
                    split(c + NSLOT)
                    if (c - c0) % 2:
                        nb = (c - c0) // 2
                        for t in range(TT):
                            act.copy(dst[:, t, 512 * nb:512 * nb + 512], ps[:, 2 * t + nb, :]).then_inc(v_evac, 1)

            for c in range(NSLOT):
                split(c)
            squares(0, lambda t: act.wait_ge(mem_in, 16))
            turned_hi(0, yT)
            act.wait_ge(x_in, 16)
            act.wait_ge(sq_pre, 2)
            squares(1, lambda t: None)
            turned_hi(1, hT)
            for j in range(4):
                evac_b(B_MEMK + j, C_MEMK + j, kmT[:, 2 * j:2 * j + 2, :])
            evac_v(C_MEMV, 4, vm)

            c = C_WIN
            act.wait_ge(used, c + 1)
            act.activation(sig, b_bank(B_WIN), ACT.Sigmoid).then_inc(b_evac, 1)
            split(c + NSLOT)
            act.wait_ge(used, c + 2)
            act.copy(glu_a, b_bank(B_WIN + 1)).then_inc(b_evac, 1)
            split(c + 1 + NSLOT)
            act.wait_ge(used, c + 3)
            act.activation(uT, b_bank(B_WIN + 2), ACT.Gelu).then_inc(b_evac, 1)
            split(c + 2 + NSLOT)
            act.wait_ge(used, c + 4)
            link(act.activation(va[:, 0, :], b_bank(B_WIN + 3)[:, 0:256], ACT.Gelu, accum_out=ln_s[:, 0:1]))
            act.activation(va[:, 1, :], b_bank(B_WIN + 3)[:, 256:512], ACT.Gelu,
                           accum_out=ln_s[:, 1:2]).then_inc(b_evac, 1)
            split(c + 3 + NSLOT)
            for t in range(TT):
                act.wait_ge(v_centered, t + 1)
                act.activation(prob[:, t, 0:256], va[:, t, :], ACT.Square, scale=1.0 / 16,
                               accum_out=ln_s[:, 4 + t:5 + t]).then_inc(v_sq, 1)
            for j in range(2):
                evac_b(B_WIN + 4 + j, c + 4 + j, qT[:, 2 * j:2 * j + 2, :])
            for j in range(2):
                evac_b(B_WIN + 6 + j, c + 6 + j, kT[:, 2 * j:2 * j + 2, :])
            for j in (8, 9):
                split(c + j + NSLOT)
            act.wait_ge(ya_raw, 1)
            act.copy(yT[0][:, 0:2, :], prob[:, 0, :].rearrange("p (a s) -> p a s", a=2)).then_inc(ya_hi, 1)
            for t in range(TT):
                act.copy(vv[:, t, 0:512], ps[:, 2 * t, :]).then_inc(v_evac, 1)

            def conv_step(s):
                if s == 4:
                    act.wait_ge(c_centered, 1)
                    act.activation(glu_a, sig, ACT.Square).then_inc(c_sq, 1)
                if s == 6:
                    act.wait_ge(c_var, 1)
                    act.activation(glu_a, ps[:, 3, :], ACT.Copy, bias=EPS).then_inc(c_eps, 1)
                if s == 8:
                    act.wait_ge(c_norm, 1)
                    for i in range(2):
                        act.activation(glu_a[:, 256 * i:256 * i + 256], sig[:, 256 * i:256 * i + 256], ACT.Silu,
                                       scale=par[:, 64 + i:65 + i], bias=par[:, 66 + i:67 + i]).then_inc(c_silu, 1)
                    act.wait_ge(c_silu, 2)
                    act.copy(yT[0][:, 6:8, :], glu_a.rearrange("p (a s) -> p a s", a=2)).then_inc(yc_hi, 1)

            def attention(kind):
                a = ATT[kind]
                n_units, u0, per, parts = a["units"], a["u0"], a["heads_per_out"], a["parts"]
                lag = 3 if kind == "diff" else 1

                def out_hi(s):
                    e = a["e0"] + s // per
                    if kind == "diff":
                        act.wait_ge(sub_on, s + 1)
                        act.copy(yT[0][:, s, :], sub_out[:, s % 2, :]).then_inc(o_hi, 1)
                        return
                    if s % per != per - 1:
                        return
                    act.wait_ge(o_ready, u0 + s + 1)
                    bank = ps[:, 6 + (e - a["e0"]) % 2, :]
                    if kind == "cross":
                        act.copy(yT[0][:, 2 * s:2 * s + 2, :],
                                 bank.rearrange("p (a s) -> p a s", a=2)).then_inc(o_hi, 1)
                    else:
                        tile = (2 if kind == "moba" else 0) + s // 2
                        act.copy(yT[0][:, tile, :], bank[:, 0:256]).then_inc(o_hi, 1)

                for s in range(n_units + (4 if kind == "diff" else 2)):
                    if s < n_units:
                        b = s % 2
                        act.wait_ge(m_ready, u0 + s + 1)
                        if s >= 2:
                            act.wait_ge(p_ready, u0 + s - 1)
                        for j in range(2 * parts):
                            if kind in ("moba", "near"):
                                src = att_bias[:, b, 256 * j:256 * j + 256]
                            elif parts == 2:
                                src = ps[:, 2 * b + j // 2, 256 * (j % 2):256 * (j % 2) + 256]
                            else:
                                src = ps[:, b, 256 * j:256 * j + 256]
                            ins = act.activation(expd[:, b, 256 * j:256 * j + 256], src, ACT.Exp,
                                                 bias=neg_top[:, b, j:j + 1],
                                                 scale=1.0 if kind == "near" else a["scale"],
                                                 accum_out=denom[:, b, j:j + 1])
                            if j == 2 * parts - 1:
                                ins.then_inc(e_ready, 1)
                    if kind == "diff" and 0 <= s - 4:
                        out_hi(s - 4)
                    if 0 <= s - 1 < n_units:
                        b = (s - 1) % 2
                        act.wait_ge(t_ready, u0 + s)
                        if s - 1 >= 2:
                            act.wait_ge(o_ready, u0 + s - 2)
                        act.copy(probT[:, b, :], ps[:, 4 + b, :]).then_inc(pt_ready, 1)
                    if kind == "diff":
                        if 0 <= s - 2 < n_units:
                            u = s - 2
                            act.wait_ge(o_ready, u0 + u + 1)
                            if u >= 2:
                                act.wait_ge(sub_ms, u - 1)
                            act.activation(sub_sq[:, u % 2, 0:256], ps[:, 6 + u % 2, 0:256],
                                           ACT.Square).then_inc(sub_sq_done, 1)
                        if 0 <= s - 3 < n_units:
                            u = s - 3
                            act.wait_ge(sub_ms, u + 1)
                            if u >= 2:
                                act.wait_ge(sub_on, u - 1)
                            act.activation(sub_sq[:, u % 2, 256:512], ps[:, 6 + u % 2, 256:512], ACT.Copy,
                                           bias=EPS).then_inc(sub_var, 1)
                    elif s - 2 >= 0:
                        out_hi(s - 2)
                    if kind == "moba":
                        conv_step(s)

            attention("moba")
            for c in range(C_WOUT, C_WOUT + 4):
                split(c + NSLOT)
            norm(0)
            for j in range(4):
                evac_b(B_XQ + j, C_XQ + j, qT[:, 2 * j:2 * j + 2, :])
            attention("cross")
            for c in range(C_XO, C_XO + 4):
                split(c + NSLOT)
            norm(1)

            act.wait_ge(used, C_RELU + 1)
            act.activation(gate, ps[:, 4, :], ACT.Relu).then_inc(gate_done, 1)
            split(C_RELU + NSLOT)
            act.wait_ge(hraw_done, 1)
            act.copy(hid[0][:, :, :], hraw.rearrange("p (a s) -> p a s", a=2)).then_inc(hid_hi, 1)
            with act.Fori(0, (RELU_BLOCKS - 1) // 3) as i:
                for j in range(3):
                    c0 = C_RELU + 1
                    act.wait_ge(used, i * 6 + (c0 + 2 * j + 1))
                    act.wait_ge(hraw_done, i * 3 + (j + 1))
                    act.activation(gate, ps[:, 4, :], ACT.Relu).then_inc(gate_done, 1)
                    split_in_loop(c0 + NSLOT + 2 * j, i, 6)
                    act.wait_ge(used, i * 6 + (c0 + 2 * j + 2))
                    act.wait_ge(hraw_done, i * 3 + (j + 2))
                    act.copy(hid[0][:, :, :], hraw.rearrange("p (a s) -> p a s", a=2)).then_inc(hid_hi, 1)
                    split_in_loop(c0 + NSLOT + 2 * j + 1, i, 6)
            split(C_LAYER - 1 + NSLOT)
            norm(2)

            def gated(c0, f):
                b0 = RELU_BLOCKS + GLU_BLOCKS * f
                act.wait_ge(used, c0 + 1)
                act.activation(gate, ps[:, 4, :], ACT.Silu).then_inc(gate_done, 1)
                split(c0 + NSLOT)
                split(c0 + 1 + NSLOT)
                act.wait_ge(hraw_done, b0 + 1)
                act.copy(hid[0][:, :, :], hraw.rearrange("p (a s) -> p a s", a=2)).then_inc(hid_hi, 1)

                def step(i):
                    c = c0 + 2
                    act.wait_ge(used, i * 3 + (c + 1))
                    act.wait_ge(hraw_done, i + (b0 + 1))
                    act.activation(gate, ps[:, 4, :], ACT.Silu).then_inc(gate_done, 1)
                    split_in_loop(c + NSLOT, i, 3)
                    split_in_loop(c + NSLOT + 1, i, 3)
                    act.wait_ge(used, i * 3 + (c + 3))
                    act.wait_ge(hraw_done, i + (b0 + 2))
                    act.copy(hid[0][:, :, :], hraw.rearrange("p (a s) -> p a s", a=2)).then_inc(hid_hi, 1)
                    split_in_loop(c + NSLOT + 2, i, 3)

                with act.Fori(0, GLU_BLOCKS - 2) as i:
                    step(i)
                step(GLU_BLOCKS - 2)
                split(c0 + 3 * GLU_BLOCKS - 1 + NSLOT)

            for layer, kind in enumerate(("diff", "near")):
                f1, cin, cout, f2 = c_layer(layer)
                gated(f1, 2 * layer)
                norm(3 + 3 * layer)
                b0 = (B_DIFF, B_NEAR)[layer]
                for j in range(8):
                    dst = (qT, kT)[j // 4]
                    evac_b(b0 + j, cin + j, dst[:, 2 * (j % 4):2 * (j % 4) + 2, :])
                evac_v(cin + 8, 4, vv)
                if layer == 0:
                    act.wait_ge(lam_dot, 2)
                    act.activation(lam[:, 2:4], lam[:, 0:2], ACT.Exp).then_inc(lam_exp, 1)
                attention(kind)
                for c in range(cout, cout + 4):
                    split(c + NSLOT)
                norm(4 + 3 * layer)
                gated(f2, 2 * layer + 1)
                norm(5 + 3 * layer)

        @block.vector
        def _(dve):
            link = linker(dve, dve_link)

            def split(c):
                if c >= N_CHUNKS:
                    return
                slot = c % NSLOT
                dve.wait_ge(hi_done, c + 1)
                dve.tensor_tensor(w_lo[:, slot, :], raw[:, slot, :], w_hi[:, slot, :],
                                  ALU.subtract).then_inc(lo_done, 1)

            def split_in_loop(c, i, per):
                if isinstance(i, int):
                    return split(c + i * per)
                slot = c % NSLOT
                dve.wait_ge(hi_done, i * per + (c + 1))
                dve.tensor_tensor(w_lo[:, slot, :], raw[:, slot, :], w_hi[:, slot, :],
                                  ALU.subtract).then_inc(lo_done, 1)

            def pre_norm(n, src, dst):
                for t in range(TT):
                    k = TT * n + t
                    dve.wait_ge(r_pre, k + 1)
                    if t == 0:
                        dve.wait_ge(gains_in[1], 16 * (n + 1))
                    dve.scalar_tensor_tensor(t1[:, t, :], src[:, t, :], rstd[:, k:k + 1], gain[:, 1, :],
                                             ALU.mult, ALU.mult).then_inc(normed, 1)
                for b in range(4):
                    t, k0 = b // 2, 4 * (b % 2)
                    dve.wait_ge(h_hi, 4 * n + b + 1)
                    part = (slice(None), slice(k0, k0 + 4), slice(t * P, (t + 1) * P))
                    dve.tensor_tensor(dst[1][part], ps[:, 4 + b, :].rearrange("p (k s) -> p k s", k=4),
                                      dst[0][part], ALU.subtract).then_inc(h_lo, 1)

            def norm(j):
                for t in range(TT):
                    k = 32 + TT * j + t
                    dve.wait_ge(r_post, TT * j + t + 1)
                    if t == 0:
                        dve.wait_ge(gains_in[0], 16 * (j + 1))
                    dve.scalar_tensor_tensor(t1[:, t, :], ps[:, 2 * t:2 * t + 2, :].rearrange("p a b -> p (a b)"),
                                             rstd[:, k:k + 1], gain[:, 0, :], ALU.mult, ALU.mult).then_inc(t1_post, 1)
                    dve.wait_ge(t1_post, TT * j + t + 1)
                    dve.scalar_tensor_tensor(x[:, t, :], t1[:, t, :], half.get(j, 1.0), x[:, t, :],
                                             ALU.mult, ALU.add).then_inc(x_new, 1)
                if j < N_NORMS - 1:
                    pre_norm(2 + j, x, hT)

            for c in range(NSLOT):
                split(c)
            dve.wait_ge(par_T, 1)
            dve.tensor_copy(par[:, 0:69], ps[:, 7, 0:69]).then_inc(par_ready, 1)
            dve.wait_ge(par_T, 2)
            dve.tensor_copy(wsT, ps[:, 6, :].rearrange("p (h t) -> p h t", h=4)).then_inc(par_ready, 1)
            dve.wait_ge(par_ready, 1)
            link(dve.tensor_scalar(par[:, 68:69], par[:, 68:69], 1.0 - LAM_INIT, None, ALU.mult))
            pre_norm(0, t1, yT)
            dve.wait_ge(turned, 4)
            pre_norm(1, x, hT)
            for c in range(C_MEMK, C_WIN):
                split(c + NSLOT)

            def conv_taps(k0, k1):
                for k in range(k0, k1):
                    for i in range(2):
                        acc = sig[:, 256 * i:256 * i + 256]
                        tap = par[:, 2 * k + i:2 * k + i + 1]
                        if k == 0:
                            dve.tensor_scalar(acc, conv_in[:, i, 0:S], tap, par[:, 62 + i:63 + i],
                                              ALU.mult, ALU.add).then_inc(conv_done, 1)
                        else:
                            dve.wait_ge(conv_done, 2 * (k - 1) + i + 1)
                            dve.scalar_tensor_tensor(acc, conv_in[:, i, k:k + S], tap, acc,
                                                     ALU.mult, ALU.add).then_inc(conv_done, 1)

            c = C_WIN
            split(c + NSLOT)
            split(c + 1 + NSLOT)
            dve.wait_ge(b_evac, B_WIN + 2)
            dve.wait_ge(const_set, 2)
            dve.tensor_tensor(conv_in[:, :, 30:30 + S], glu_a.rearrange("p (i s) -> p i s", i=2),
                              sig.rearrange("p (i s) -> p i s", i=2), ALU.mult).then_inc(glu_ready, 1)
            dve.wait_ge(glu_ready, 1)
            conv_taps(0, 4)
            split(c + 2 + NSLOT)
            conv_taps(4, 8)
            split(c + 3 + NSLOT)
            dve.wait_ge(b_evac, B_WIN + 4)
            dve.wait_ge(small_in, 16 * 18)
            link(dve.tensor_scalar(ln_s[:, 2:4], ln_s[:, 0:2], 1.0 / 256, None, ALU.mult))
            for t in range(TT):
                dve.tensor_scalar(va[:, t, :], va[:, t, :], ln_s[:, 2 + t:3 + t], None,
                                  ALU.subtract).then_inc(v_centered, 1)
            conv_taps(8, 10)
            for t in range(TT):
                dve.wait_ge(v_r, t + 1)
                link(dve.scalar_tensor_tensor(va[:, t, :], va[:, t, :], ln_s[:, 6 + t:7 + t], ln_g,
                                              ALU.mult, ALU.mult))
                dve.tensor_tensor(va[:, t, :], va[:, t, :], ln_b, ALU.add).then_inc(v_normed, 1)
            for j in range(4, 8):
                split(c + j + NSLOT)
                conv_taps(4 * j - 6, 4 * j - 2)
            dve.wait_ge(mix_ready, 1)
            link(dve.tensor_tensor(prob[:, 1, :], ps[:, 6, :], b_mix.rearrange("p a s -> p (a s)"), ALU.add))
            dve.tensor_tensor(prob[:, 0, :], prob[:, 1, :], uT, ALU.mult).then_inc(ya_raw, 1)
            split(c + 8 + NSLOT)
            split(c + 9 + NSLOT)
            dve.wait_ge(ya_hi, 1)
            dve.tensor_tensor(yT[1][:, 0:2, :], prob[:, 0, :].rearrange("p (a s) -> p a s", a=2), yT[0][:, 0:2, :],
                              ALU.subtract).then_inc(ya_lo, 1)
            dve.wait_ge(ya_lo, 1)
            conv_taps(26, 31)

            def conv_step(s):
                if s == 3:
                    dve.wait_ge(cm_ready, 1)
                    dve.tensor_tensor(sig, sig, ps[:, 2, :], ALU.subtract).then_inc(c_centered, 1)
                if s == 7:
                    dve.wait_ge(c_r, 2)
                    dve.tensor_tensor(sig, sig, glu_a, ALU.mult).then_inc(c_norm, 1)
                if s == 9:
                    dve.wait_ge(yc_hi, 1)
                    dve.tensor_tensor(yT[1][:, 6:8, :], glu_a.rearrange("p (a s) -> p a s", a=2), yT[0][:, 6:8, :],
                                      ALU.subtract).then_inc(yc_lo, 1)

            def attention(kind):
                a = ATT[kind]
                n_units, u0, per, parts = a["units"], a["u0"], a["heads_per_out"], a["parts"]
                n = 2 * parts

                def scores_max(s):
                    b = s % 2
                    dve.wait_ge(s_ready, u0 + s + 1)
                    if s >= 2:
                        dve.wait_ge(e_ready, u0 + s - 1)
                    if kind == "moba":
                        slope = 2.0 ** -(s + 1)
                        link(dve.scalar_tensor_tensor(att_bias[:, b, :], dist, -slope / a["scale"], ps[:, b, :],
                                                      ALU.mult, ALU.add))
                        src = att_bias[:, b, :].rearrange("p (j s) -> p j s", j=n)
                    elif kind == "near":
                        if s == 0:
                            dve.wait_ge(bias_masked, 16)
                        for t in range(TT):
                            ins = dve.scalar_tensor_tensor(
                                att_bias[:, b, 256 * t:256 * t + 256].rearrange("p (j c) -> p j c", j=4),
                                ps[:, b, 256 * t:256 * t + 256].rearrange("p (j c) -> p j c", j=4), a["scale"],
                                bias[:, s, 2 - 2 * t:6 - 2 * t, :], ALU.mult, ALU.add)
                        link(ins)
                        src = att_bias[:, b, :].rearrange("p (j s) -> p j s", j=n)
                    elif parts == 2:
                        src = ps[:, 2 * b:2 * b + 2, :].rearrange("p a (j s) -> p (a j) s", j=2)
                    else:
                        src = ps[:, b, :].rearrange("p (j s) -> p j s", j=n)
                    link(dve.tensor_reduce(top[:, b, 0:n], src, AX_X, ALU.max))
                    dve.tensor_scalar(neg_top[:, b, 0:n], top[:, b, 0:n],
                                      -1.0 if kind == "near" else -a["scale"], None, ALU.mult).then_inc(m_ready, 1)

                def normalise(u):
                    b = u % 2
                    dve.wait_ge(e_ready, u0 + u + 1)
                    link(dve.reciprocal(inv_denom[:, b, 0:n], denom[:, b, 0:n]))
                    if u >= 2:
                        dve.wait_ge(t_ready, u0 + u - 1)
                    if parts == 2:
                        link(dve.tensor_scalar(inv_denom[:, b, 2:4], inv_denom[:, b, 2:4], lam[:, 4:5], None, ALU.mult))
                    for t in range(TT):
                        ins = dve.tensor_scalar(prob[:, b, 256 * t:256 * t + 256], expd[:, b, 256 * t:256 * t + 256],
                                                inv_denom[:, b, t:t + 1], None, ALU.mult)
                    if parts == 2:
                        link(ins)
                        for t in range(TT):
                            dst = prob[:, b, 256 * t:256 * t + 256]
                            ins = dve.scalar_tensor_tensor(dst, expd[:, b, 512 + 256 * t:768 + 256 * t],
                                                           inv_denom[:, b, 2 + t:3 + t], dst, ALU.mult, ALU.add)
                    ins.then_inc(p_ready, 1)

                def sub_norm(u):
                    dve.wait_ge(sub_r, u + 1)
                    if u >= 2:
                        dve.wait_ge(o_lo, a["e0"] + u - 1)
                    dve.scalar_tensor_tensor(sub_out[:, u % 2, :], ps[:, 6 + u % 2, 0:256], par[:, 68:69],
                                             sub_sq[:, u % 2, 256:512], ALU.mult, ALU.mult).then_inc(sub_on, 1)

                def out_lo(u):
                    if u % per != per - 1:
                        return
                    e = u // per
                    dve.wait_ge(o_hi, a["e0"] + e + 1)
                    bank = ps[:, 6 + e % 2, :]
                    if kind == "diff":
                        tiles, src = slice(u, u + 1), sub_out[:, u % 2, :].rearrange("p (a s) -> p a s", a=1)
                    elif kind == "cross":
                        tiles, src = slice(2 * u, 2 * u + 2), bank.rearrange("p (a s) -> p a s", a=2)
                    else:
                        tile = (2 if kind == "moba" else 0) + e
                        tiles, src = slice(tile, tile + 1), bank[:, 0:256].rearrange("p (a s) -> p a s", a=1)
                    dve.tensor_tensor(yT[1][:, tiles, :], src, yT[0][:, tiles, :], ALU.subtract).then_inc(o_lo, 1)

                for s in range(n_units + (4 if kind == "diff" else 2)):
                    if kind == "diff" and s >= 4:
                        sub_norm(s - 4)
                    if s < n_units:
                        scores_max(s)
                    if 0 <= s - 1 < n_units:
                        normalise(s - 1)
                    if kind == "diff":
                        if s >= 4:
                            out_lo(s - 4)
                    elif s >= 2:
                        out_lo(s - 2)
                    if kind == "moba":
                        conv_step(s)

            attention("moba")
            for c in range(C_WOUT, C_WOUT + 4):
                split(c + NSLOT)
            norm(0)
            for c in range(C_XQ, C_XQ + 4):
                split(c + NSLOT)
            attention("cross")
            for c in range(C_XO, C_XO + 4):
                split(c + NSLOT)
            norm(1)

            def hidden_lo(n):
                dve.wait_ge(hid_hi, n)
                dve.tensor_tensor(hid[1][:, :, :], hraw.rearrange("p (a s) -> p a s", a=2), hid[0][:, :, :],
                                  ALU.subtract).then_inc(hid_lo, 1)

            dve.wait_ge(gate_done, 1)
            dve.scalar_tensor_tensor(hraw, ps[:, 4, :], 0.0, gate, ALU.max, ALU.mult).then_inc(hraw_done, 1)
            split(C_RELU + NSLOT)
            hidden_lo(1)
            with dve.Fori(0, (RELU_BLOCKS - 1) // 3) as i:
                for j in range(3):
                    c = C_RELU + 1 + 2 * j
                    dve.wait_ge(gate_done, i * 3 + (j + 2))
                    dve.wait_ge(hid_lo, i * 3 + (j + 1))
                    dve.scalar_tensor_tensor(hraw, ps[:, 4, :], 0.0, gate,
                                             ALU.max, ALU.mult).then_inc(hraw_done, 1)
                    split_in_loop(c + NSLOT, i, 6)
                    hidden_lo(i * 3 + (j + 2))
                    split_in_loop(c + 1 + NSLOT, i, 6)
            split(C_LAYER - 1 + NSLOT)
            norm(2)

            def gated(c0, f):
                b0 = g0 = RELU_BLOCKS + GLU_BLOCKS * f
                split(c0 + NSLOT)
                dve.wait_ge(gate_done, g0 + 1)
                dve.wait_ge(used, c0 + 2)
                dve.tensor_tensor(hraw, gate, ps[:, 5, :], ALU.mult).then_inc(hraw_done, 1)
                split(c0 + 1 + NSLOT)
                hidden_lo(b0 + 1)

                def step(i):
                    c = c0 + 2
                    split_in_loop(c + NSLOT, i, 3)
                    dve.wait_ge(gate_done, i + (g0 + 2))
                    dve.wait_ge(used, i * 3 + (c + 2))
                    dve.wait_ge(hid_lo, i + (b0 + 1))
                    dve.tensor_tensor(hraw, gate, ps[:, 5, :], ALU.mult).then_inc(hraw_done, 1)
                    split_in_loop(c + NSLOT + 1, i, 3)
                    hidden_lo(i + (b0 + 2))
                    split_in_loop(c + NSLOT + 2, i, 3)

                with dve.Fori(0, GLU_BLOCKS - 2) as i:
                    step(i)
                step(GLU_BLOCKS - 2)
                split(c0 + 3 * GLU_BLOCKS - 1 + NSLOT)

            def rope(j):
                dst = (qT, kT)[j // 4][:, 2 * (j % 4):2 * (j % 4) + 2, :]
                sin2, cos2 = (m.rearrange("p (a s) -> p a s", a=1).broadcast_to([P, 2, S]) for m in (sin, cos))
                part = rope_t.rearrange("p (a s) -> p a s", a=2)
                dve.wait_ge(rot_ready, j + 1)
                if j:
                    dve.wait_ge(rope_done, j)
                dve.tensor_tensor(part, ps[:, 6 + j % 2, :].rearrange("p (a s) -> p a s", a=2), sin2,
                                  ALU.mult).then_inc(rope_mul, 1)
                link(dve.tensor_tensor(dst, dst, cos2, ALU.mult))
                dve.wait_ge(rope_mul, j + 1)
                dve.tensor_tensor(dst, dst, part, ALU.add).then_inc(rope_done, 1)

            for layer, kind in enumerate(("diff", "near")):
                f1, cin, cout, f2 = c_layer(layer)
                gated(f1, 2 * layer)
                norm(3 + 3 * layer)
                for j in range(12):
                    split(cin + j + NSLOT)
                    if layer == 0 and 1 <= j <= 8:
                        rope(j - 1)
                if layer == 0:
                    for j in range(2):
                        dve.tensor_tensor_reduce(sub_out[:, j, 0:64], lam_rows[:, 2 * j, :],
                                                 lam_rows[:, 2 * j + 1, :], 1.0, 0.0, ALU.mult, ALU.add,
                                                 lam[:, j:j + 1]).then_inc(lam_dot, 1)
                    dve.wait_ge(lam_exp, 1)
                    link(dve.tensor_tensor(lam[:, 5:6], lam[:, 3:4], lam[:, 2:3], ALU.subtract))
                    link(dve.tensor_scalar(lam[:, 4:5], lam[:, 5:6], LAM_INIT, None, ALU.subtract))
                attention(kind)
                for c in range(cout, cout + 4):
                    split(c + NSLOT)
                norm(4 + 3 * layer)
                gated(f2, 2 * layer + 1)
                norm(5 + 3 * layer)

        @block.tensor
        def _(pe):
            def transposed_product(src, slot, bank):
                wh, wl = (m[:, slot, :].rearrange("p (k n) -> p k n", k=KT) for m in (w_hi, w_lo))
                for n in range(2):
                    o = bank[:, 256 * n:256 * n + 256]
                    for k in range(KT):
                        hi, lo = wh[:, k, 128 * n:128 * n + 128], wl[:, k, 128 * n:128 * n + 128]
                        pe.matmul(o, hi, src[0][:, k, :], start=(k == 0), stop=False)
                        pe.matmul(o, hi, src[1][:, k, :], start=False, stop=False)
                        ins = pe.matmul(o, lo, src[0][:, k, :], start=False, stop=(k == KT - 1))
                return ins

            def rows_product(src, tiles, slot, width, banks, first, last, half_sem=None):
                wh, wl = (m[:, slot, :].rearrange("p (k n) -> p k n", k=len(tiles)) for m in (w_hi, w_lo))
                for t in range(TT):
                    for nb in range(len(banks[t])):
                        o = banks[t][nb]
                        cols = slice(width * nb, width * nb + width)
                        for i, k in enumerate(tiles):
                            hi, lo = (m[:, k, t * P:(t + 1) * P] for m in src)
                            pe.matmul(o, hi, wh[:, i, cols], start=first and i == 0, stop=False)
                            pe.matmul(o, hi, wl[:, i, cols], start=False, stop=False)
                            ins = pe.matmul(o, lo, wh[:, i, cols], start=False, stop=last and i == len(tiles) - 1)
                    if t == 0 and half_sem is not None:
                        ins.then_inc(half_sem, 1)
                return ins

            def b_product(n, c, src):
                pe.wait_ge(lo_done, c + 1)
                if n >= 2:
                    pe.wait_ge(b_evac, n - 1)
                transposed_product(src, c % NSLOT, b_bank(n)).then_inc(used, 1)

            def a_product(c0, j, src, y_for_norm=False):
                c = c0 + j
                pe.wait_ge(lo_done, c + 1)
                nb, kh = j // 2, j % 2
                banks = [[ps[:, 2 * t + nb, :]] for t in range(TT)]
                rows_product(src, range(4 * kh, 4 * kh + 4), c % NSLOT, 512, banks, kh == 0, kh == 1,
                             y_half if y_for_norm and j == 3 else None).then_inc(used, 1)

            def turn(n):
                for t in range(TT):
                    pe.wait_ge(normed, TT * n + t + 1)
                    for b in range(2):
                        for k in range(4):
                            col = P * (4 * b + k)
                            ins = pe.transpose(ps[:, 4 + 2 * t + b, k * P:(k + 1) * P], t1[:, t, col:col + P], ident)
                        ins.then_inc(turned, 1)

            pe.wait_ge(tab_in, 16)
            pe.wait_ge(masked, 1)
            pe.transpose(ps[:, 7, 0:69], par_rows[:, :], ident[0:69, 0:69]).then_inc(par_T, 1)
            for h in range(4):
                ins = pe.transpose(ps[:, 6, h * P:(h + 1) * P], ws_raw[:, h, :], ident)
            ins.then_inc(par_T, 1)
            pe.wait_ge(par_ready, 2)
            turn(0)
            pe.wait_ge(h_lo, 4)
            turn(1)
            pe.wait_ge(h_lo, 8)
            for j in range(4):
                b_product(B_MEMK + j, C_MEMK + j, yT)
            for j in range(4):
                a_product(C_MEMV, j, yT)
            for j in range(3):
                b_product(B_WIN + j, C_WIN + j, hT)
            c, n = C_WIN + 3, B_WIN + 3
            pe.wait_ge(lo_done, c + 1)
            pe.wait_ge(b_evac, n - 1)
            rows_product(hT, range(KT), c % NSLOT, 256,
                         [[b_bank(n)[:, 256 * t:256 * t + 256]] for t in range(TT)], True, True).then_inc(used, 1)
            for j in range(4, 8):
                b_product(B_WIN + j, C_WIN + j, hT)
            pe.wait_ge(v_normed, TT)
            for h in range(4):
                for t in range(TT):
                    rows = slice(64 * (h % 2), 64 * (h % 2) + 64)
                    col = 256 * (h // 2) + t * P
                    ins = pe.matmul(ps[rows, 6, col:col + P], va[:, t, 64 * h:64 * h + 64], wsT[:, h, :],
                                    start=True, stop=True)
            ins.then_inc(mix_ready, 1)
            pe.wait_ge(v_evac, TT * 2)
            for j in range(2):
                a_product(C_WIN + 8, j, hT)

            def conv_step(s):
                if s == 2:
                    pe.wait_ge(conv_done, 62)
                    pe.matmul(ps[:, 2, :], group_mean, sig, start=True, stop=True).then_inc(cm_ready, 1)
                if s == 5:
                    pe.wait_ge(c_sq, 1)
                    pe.matmul(ps[:, 3, :], group_mean, glu_a, start=True, stop=True).then_inc(c_var, 1)

            def attention(kind):
                a = ATT[kind]
                n_units, u0, per, parts = a["units"], a["u0"], a["heads_per_out"], a["parts"]

                def scores(s):
                    b = s % 2
                    if s >= 2:
                        pe.wait_ge(e_ready, u0 + s - 1)
                    for part in range(parts):
                        bank = ps[:, 2 * b + part if parts == 2 else b, :]
                        for t in range(TT):
                            o = bank[:, 256 * t:256 * t + 256]
                            if kind == "cross":
                                for i in range(2):
                                    ins = pe.matmul(o, qT[:, 2 * s + i, t * P:(t + 1) * P], kmT[:, 2 * s + i, :],
                                                    start=(i == 0), stop=(i == 1))
                            else:
                                head = 2 * s + part if parts == 2 else s
                                rows = slice(64 * (head % 2), 64 * (head % 2) + 64)
                                ins = pe.matmul(o, qT[rows, head // 2, t * P:(t + 1) * P], kT[rows, head // 2, :],
                                                start=True, stop=True)
                    ins.then_inc(s_ready, 1)

                def turn_prob(u):
                    b = u % 2
                    pe.wait_ge(p_ready, u0 + u + 1)
                    if u >= 2:
                        pe.wait_ge(pt_ready, u0 + u - 1)
                    for kt in range(TT):
                        for t in range(TT):
                            ins = pe.transpose(ps[:, 4 + b, 256 * kt + t * P:256 * kt + (t + 1) * P],
                                               prob[:, b, 256 * t + kt * P:256 * t + (kt + 1) * P], ident)
                    ins.then_inc(t_ready, 1)

                def weigh_values(u):
                    b, e = u % 2, u // per
                    pe.wait_ge(pt_ready, u0 + u + 1)
                    if e >= 2:
                        if kind == "diff":
                            pe.wait_ge(sub_on, e - 1)
                        else:
                            pe.wait_ge(o_lo, a["e0"] + e - 1)
                    values = vm if kind == "cross" else vv
                    bank = ps[:, 6 + e % 2, :]
                    for et in range(2 if kind == "cross" else 1):
                        if kind in ("moba", "near"):
                            o, cols = bank[64 * (u % 2):64 * (u % 2) + 64, 0:256], slice(64 * u, 64 * u + 64)
                        elif kind == "cross":
                            o, cols = bank[:, 256 * et:256 * et + 256], slice(256 * u + P * et, 256 * u + P * et + P)
                        else:
                            o, cols = bank[:, 0:256], slice(P * u, P * u + P)
                        for kt in range(TT):
                            ins = pe.matmul(o, values[:, kt, cols], probT[:, b, 256 * kt:256 * kt + 256],
                                            start=(kt == 0), stop=(kt == TT - 1))
                    ins.then_inc(o_ready, 1)

                for s in range(n_units + (3 if kind == "diff" else 2)):
                    if s < n_units:
                        scores(s)
                    if 0 <= s - 1 < n_units:
                        turn_prob(s - 1)
                    if 0 <= s - 2 < n_units:
                        weigh_values(s - 2)
                    if kind == "diff" and s >= 3:
                        u = s - 3
                        pe.wait_ge(sub_sq_done, u + 1)
                        pe.matmul(ps[:, 6 + u % 2, 256:512], all_mean, sub_sq[:, u % 2, 0:256],
                                  start=True, stop=True).then_inc(sub_ms, 1)
                    if kind == "moba":
                        conv_step(s)

            pe.wait_ge(v_evac, TT * 2 + TT)
            pe.wait_ge(ya_raw, 1)
            attention("moba")
            pe.wait_ge(ya_lo, 1)
            pe.wait_ge(yc_lo, 1)
            pe.wait_ge(o_lo, 4)
            for j in range(4):
                a_product(C_WOUT, j, yT, True)
            turn(2)
            pe.wait_ge(h_lo, 12)
            for j in range(4):
                b_product(B_XQ + j, C_XQ + j, hT)
            pe.wait_ge(b_evac, B_XQ + 4)
            attention("cross")
            pe.wait_ge(o_lo, 8)
            for j in range(4):
                a_product(C_XO, j, yT, True)
            turn(3)
            pe.wait_ge(h_lo, 16)

            def down(c, i, per, blocks, first, last):
                pe.wait_ge(lo_done, i * per + (c + 1))
                pe.wait_ge(hid_lo, blocks)
                banks = [[ps[:, 2 * t + nb, :] for nb in range(2)] for t in range(TT)]
                rows_product(hid, range(2), c % NSLOT, 512, banks, first, last,
                             y_half if last else None).then_inc(used, 1)

            def up(c, i, per, bank):
                pe.wait_ge(lo_done, i * per + (c + 1))
                transposed_product(hT, c % NSLOT, ps[:, bank, :]).then_inc(used, 1)

            def relu_steps(i, opens):
                for j in range(3):
                    c = C_RELU + 1 + 2 * j
                    pe.wait_ge(hraw_done, i * 3 + (j + 1))
                    up(c, i, 6, 4)
                    down(c + 1, i, 6, i * 3 + (j + 1), opens and j == 0, False)

            up(C_RELU, 0, 0, 4)
            relu_steps(0, True)
            with pe.Fori(1, (RELU_BLOCKS - 1) // 3) as i:
                relu_steps(i, False)
            down(C_LAYER - 1, 0, 0, RELU_BLOCKS, False, True)
            turn(4)
            pe.wait_ge(h_lo, 20)

            def gated(c0, f):
                b0 = g0 = RELU_BLOCKS + GLU_BLOCKS * f

                def step(i, opens):
                    c = c0 + 2
                    pe.wait_ge(gate_done, i + (g0 + 1))
                    up(c, i, 3, 4)
                    pe.wait_ge(hraw_done, i + (b0 + 1))
                    up(c + 1, i, 3, 5)
                    down(c + 2, i, 3, i + (b0 + 1), opens, False)

                up(c0, 0, 0, 4)
                up(c0 + 1, 0, 0, 5)
                step(0, True)
                with pe.Fori(1, GLU_BLOCKS - 1) as i:
                    step(i, False)
                down(c0 + 3 * GLU_BLOCKS - 1, 0, 0, b0 + GLU_BLOCKS, False, True)

            for layer, kind in enumerate(("diff", "near")):
                f1, cin, cout, f2 = c_layer(layer)
                gated(f1, 2 * layer)
                turn(5 + 3 * layer)
                pe.wait_ge(h_lo, 4 * (6 + 3 * layer))
                n0 = (B_DIFF, B_NEAR)[layer]

                def rotate(j):
                    pe.wait_ge(b_evac, n0 + j + 1)
                    if j >= 2:
                        pe.wait_ge(rope_mul, j - 1)
                    for n in range(2):
                        ins = pe.matmul(ps[:, 6 + j % 2, 256 * n:256 * n + 256], rot,
                                        (qT, kT)[j // 4][:, 2 * (j % 4) + n, :], start=True, stop=True)
                    ins.then_inc(rot_ready, 1)

                for j in range(8):
                    b_product(n0 + j, cin + j, hT)
                    if layer == 0 and j:
                        rotate(j - 1)
                for j in range(4):
                    a_product(cin + 8, j, hT)
                    if layer == 0 and j == 0:
                        rotate(7)
                pe.wait_ge(b_evac, n0 + 8)
                if layer == 0:
                    pe.wait_ge(rope_done, 8)
                pe.wait_ge(v_evac, TT * (5 + 2 * layer))
                attention(kind)
                pe.wait_ge(o_lo, (16, 24)[layer])
                for j in range(4):
                    a_product(cout, j, yT, True)
                turn(6 + 3 * layer)
                pe.wait_ge(h_lo, 4 * (7 + 3 * layer))
                gated(f2, 2 * layer + 1)
                if layer == 0:
                    turn(7)
                    pe.wait_ge(h_lo, 32)


_UNUSED = ("gqa_w_in_2", "gqa_w_out_2", "gqa_qk_norm_2")


def kernel(**inputs):
    import concourse.bacc as bacc
    from concourse.bass_utils import run_bass_kernel_spmd

    nc = bacc.Bacc("TRN2", target_bir_lowering=False, num_devices=1)
    arrays, w = {}, {}
    for name, value in inputs.items():
        if name in _UNUSED:
            continue
        arrays[name] = np.ascontiguousarray(value)
        w[name] = nc.dram_tensor(name, arrays[name].shape, mybir.dt.from_np(arrays[name].dtype),
                                 kind="ExternalInput").ap()
    arrays["shape_tables"] = shape_tables()
    table = nc.dram_tensor("shape_tables", arrays["shape_tables"].shape, F32, kind="ExternalInput").ap()
    out = nc.dram_tensor("result", [1, S, D], F32, kind="ExternalOutput").ap()
    build(nc, w, table, out)
    r = run_bass_kernel_spmd(nc, [arrays], core_ids=[0])
    return r.results[0]["result"]
```

```python
from contextlib import ExitStack

import numpy as np

import concourse.bass as bass
from concourse import mybir

F32 = mybir.dt.float32
F32R = mybir.dt.float32r
ACT = mybir.ActivationFunctionType
ALU = mybir.AluOpType
AX_X = mybir.AxisListType.X

P = 128
D = 1024
S = 256
KT = D // P
TT = S // P
EPS = 1e-6
NSLOT = 3
CH = 2048
FF1, FF2 = 4096, 2816
RELU_BLOCKS = FF1 // 256
GLU_BLOCKS = FF2 // 256
FAR = 1e30

C_MIX = 0
C_CROSS = C_MIX + 22
C_RELU = C_CROSS + 8
C_LAYER = C_RELU + 2 * RELU_BLOCKS
PER_LAYER = 2 * 3 * GLU_BLOCKS + 16
N_CHUNKS = C_LAYER + 2 * PER_LAYER


def c_layer(layer):
    c = C_LAYER + layer * PER_LAYER
    return c, c + 3 * GLU_BLOCKS, c + 3 * GLU_BLOCKS + 16


ATT = {
    "moba": dict(units=8, u0=0, e0=0, per_out=2, scale=0.125, parts=1, per_chunk=4, steps=10),
    "cross": dict(units=4, u0=8, e0=4, per_out=1, scale=1.0 / 16, parts=1, per_chunk=1, steps=6),
    "diff": dict(units=8, u0=12, e0=8, per_out=1, scale=0.125, parts=2, per_chunk=2, steps=11),
    "near": dict(units=16, u0=20, e0=16, per_out=2, scale=0.125, parts=1, per_chunk=4, steps=18),
}

PLAN = {
    "moba": ("g0 a0 mem glu consts u0 taps0 w0 gate_norm taps1 K0 taps2 K1 gate_scale taps3 K2 mix taps4 K3 mix_raw "
             "taps5 V0 taps6 V1 taps7 V2 conv_mean V3 conv_var mix_out q0 conv_root k0 conv_out v0 "
             "0 q1 1 k1 2 v1 3 o0 4 5 o3 6 7 o1 8 9 o2"),
    "cross": "q0 q1 0 q2 1 q3 2 3 o0 4 o1 5 o2 o3",
    "diff": ("q0 k0 rot0 v0 rot4 lambda q1 0 k1 1 rot1 v1 rot5 q2 2 k2 3 rot2 v2 rot6 q3 4 k3 5 rot3 v3 rot7 "
             "6 o0 7 o1 8 o2 9 10 o3"),
    "near": "q0 k0 v0 0 q1 1 k1 2 v1 3 4 q2 5 k2 6 v2 7 8 q3 9 k3 10 v3 11 12 o0 13 14 o1 15 o2 16 17 o3",
}
STAGES = {"moba": (C_MIX, 0), "cross": (C_CROSS, 18), "diff": (c_layer(0)[1], 22), "near": (c_layer(1)[1], 34)}


def plan(kind):
    c, n = STAGES[kind]
    for word in PLAN[kind].split():
        if len(word) == 2 and word[0].isalpha():
            yield word[0], int(word[1]), c, n
            c += 1
            n += word[0] != "o"
        elif word.isdigit():
            yield "step", int(word), None, None
        else:
            name = word.rstrip("0123456789")
            yield name, int(word[len(name):] or 0), None, None


def product_number(kind, letter, digit):
    return [n for name, d, _, n in plan(kind) if (name, d) == (letter, digit)][0]


def products_of(kind, s):
    a = ATT[kind]
    number = {(name, digit): n for name, digit, _, n in plan(kind)}
    heads = []
    if s < a["units"]:
        heads += [(letter, s // a["per_chunk"]) for letter in "qk"]
    if s >= 2:
        heads.append(("v", (s - 2) // a["per_chunk"]))
    return 1 + max(number.get(head, 0) for head in heads)


N_SMALL = 14
LAM_INIT = 0.8 - 0.6 * float(np.exp(-0.3 * 0))


def shape_tables():
    t = np.arange(S)
    q = np.arange(P)
    dist = np.zeros((P, TT, S), np.float32)
    for tt in range(TT):
        d = (tt * P + q)[:, None] - t[None, :]
        dist[:, tt] = np.where(d >= 0, d, FAR)
    ident = np.eye(P, dtype=np.float32)
    group = np.kron(np.eye(2), np.ones((64, 64))).astype(np.float32) / np.float32(64)
    mean = np.full((P, P), 1 / P, np.float32)
    rot = np.zeros((P, P), np.float32)
    inv = np.float32(500000.0) ** (-np.arange(0, 16, 2, dtype=np.float32) / np.float32(16))
    ang = (t.astype(np.float32)[:, None] * inv[None, :].astype(np.float32)).astype(np.float32)
    cos = np.ones((P, S), np.float32)
    sin = np.zeros((P, S), np.float32)
    for base in (0, 64):
        for j in range(8):
            rot[base + j + 8, base + j] = -1.0
            rot[base + j, base + j + 8] = 1.0
            for o in (0, 8):
                cos[base + j + o] = np.cos(ang[:, j])
                sin[base + j + o] = np.sin(ang[:, j])
    col = np.arange(64)
    start = np.clip(col - 8, 0, 48)
    inside = (col[None, :] >= start[:, None]) & (col[None, :] < start[:, None] + 16)
    window = np.tile(np.where(inside, 0.0, -FAR).astype(np.float32), (2, 1))
    return np.concatenate([ident, group, mean, rot, cos, sin, window, dist.reshape(P, -1)], axis=1)


TABLE_COLS = 4 * P + 2 * S + 64


def build(nc, w, table, out):
    with ExitStack() as ctx:
        def sb(name, shape, dt=F32):
            return ctx.enter_context(nc.sbuf_tensor(name, shape, dt))

        def sem(name):
            return ctx.enter_context(nc.semaphore(name))

        raw = sb("raw", [P, NSLOT, CH])
        w_hi = sb("w_hi", [P, NSLOT, CH], F32R)
        w_lo = sb("w_lo", [P, NSLOT, CH], F32R)
        x = sb("x_rows", [P, TT, D])
        t1 = sb("t1", [P, TT, D])
        hT = (sb("hT_hi", [P, KT, S], F32R), sb("hT_lo", [P, KT, S], F32R))
        yT = (sb("yT_hi", [P, KT, S], F32R), sb("yT_lo", [P, KT, S], F32R))
        hid = (sb("hid_hi", [P, 2, S], F32R), sb("hid_lo", [P, 2, S], F32R))
        qT = sb("qT", [P, KT, S])
        kT = sb("kT", [P, KT, S])
        vv = sb("vv", [P, TT, D])
        big = sb("big", [P, 3 * CH])
        kmT = big[:, 0:CH].rearrange("p (k s) -> p k s", k=KT)
        vm = big[:, CH:2 * CH].rearrange("p (t d) -> p t d", t=TT)
        uT = big[:, 2 * CH:2 * CH + 512]
        va = big[:, 2 * CH + 512:2 * CH + 1024].rearrange("p (t d) -> p t d", t=TT)
        sig = big[:, 2 * CH + 1024:2 * CH + 1536]
        glu_a = big[:, 2 * CH + 1536:3 * CH]
        bias = big[:, :].rearrange("p (h j c) -> p h j c", h=16, j=6)
        conv_in = qT[:, 4:7, :].rearrange("p a b -> p (a b)")[:, 0:2 * 286].rearrange("p (i t) -> p i t", i=2)
        b_mix = kT[:, 4:6, :]
        ln_g = kT[:, 6, :]
        ln_b = kT[:, 7, :]
        wsT = vv[:, 0, 512:1024].rearrange("p (h t) -> p h t", h=4)
        dist = vv[:, 1, 512:1024]
        gain = sb("gain", [P, 2, D])
        att_bias = sb("att_bias", [P, 2, 512])
        prob = sb("prob", [P, 2, 512])
        probT = sb("probT", [P, 2, 512])
        expd = t1[:, :, :]
        ws_raw = att_bias[:, 0, :].rearrange("p (h t) -> p h t", h=4)
        tab = sb("tab", [P, TABLE_COLS])
        ident = tab[:, 0:P]
        group_mean = tab[:, P:2 * P]
        all_mean = tab[:, 2 * P:3 * P]
        rot = tab[:, 3 * P:4 * P]
        cos = tab[:, 4 * P:4 * P + S]
        sin = tab[:, 4 * P + S:4 * P + 2 * S]
        window = tab[:, 4 * P + 2 * S:TABLE_COLS]
        par_rows = sb("par_rows", [68, P])
        par = sb("par", [P, 68])
        lam_rows = sb("lam_rows", [P, 4, 64])
        sub_gain = sb("sub_gain", [P, P])
        lam = sb("lam", [P, 8])
        minus_half = sb("minus_half", [P, 2])
        ssq = sb("ssq", [P, 64])
        rstd = sb("rstd", [P, 64])
        top = sb("top", [P, 2, 4])
        neg_top = sb("neg_top", [P, 2, 4])
        denom = sb("denom", [P, 2, 4])
        inv_denom = sb("inv_denom", [P, 2, 4])
        ln_s = sb("ln_s", [P, 8])
        hraw = t1[:, 0, 0:512]
        gate = t1[:, 0, 512:1024]
        rope_t = sb("rope_t", [P, 512])
        sub_dump = att_bias
        sub_out = sb("sub_out", [P, 2, S])
        gated_u = sub_out[:, :, :].rearrange("p a s -> p (a s)")
        sub_stat = sb("sub_stat", [P, 2, 4])
        eps_col = sb("eps_col", [P, 1])
        mem_rows = big[:, CH:2 * CH].rearrange("p (t d) -> p t d", t=TT)

        ps = ctx.enter_context(nc.psum_tensor("ps", [P, 8, 512], F32))

        landed = [sem(f"chunk_landed_{s}") for s in range(NSLOT)]
        hi_done, lo_done, used = sem("hi_done"), sem("lo_done"), sem("chunk_used")
        gains_in = [sem("gain_post_in"), sem("gain_pre_in")]
        x_in, mem_in, tab_in, small_in = sem("x_in"), sem("mem_in"), sem("tab_in"), sem("small_in")
        bias_in, out_done = sem("bias_in"), sem("out_done")
        masked, const_set = sem("ws_masked"), sem("const_set")
        par_T, par_ready = sem("par_transposed"), sem("par_ready")
        y_half, sq_post, r_post, t1_post, x_new = (sem(n) for n in ("y_half", "sq_post", "r_post", "t1_post", "x_new"))
        sq_pre, r_pre, normed, turned, h_hi, h_lo = (sem(n) for n in ("sq_pre", "r_pre", "normed", "turned", "h_hi", "h_lo"))
        b_evac = sem("b_evac")
        gate_done, hraw_done, hid_hi, hid_lo = (sem(n) for n in ("gate_done", "hraw_done", "hid_hi_done", "hid_lo_done"))
        s_ready, m_ready, e_ready, p_ready, t_ready, pt_ready, o_ready, o_hi, o_lo = (
            sem(n) for n in ("scores_ready", "max_ready", "exp_ready", "prob_ready", "probT_turned", "probT_ready",
                             "out_ready", "out_hi", "out_lo"))
        rot_ready, rope_mul, rope_done = sem("rot_ready"), sem("rope_mul"), sem("rope_done")
        sub_sq_done, sub_r, sub_on, sub_turned = (sem(n) for n in ("sub_sq", "sub_r", "sub_on", "sub_turned"))
        v_centered, v_sq, v_r, v_normed, mix_ready, ya_raw, glu_ready, conv_done = (
            sem(n) for n in ("v_centered", "v_sq", "v_r", "v_normed", "mix_ready", "ya_raw", "glu_ready", "conv_done"))
        cm_ready, c_centered, c_sq, c_var, c_root, c_norm, c_silu, yc_hi, yc_lo, ya_hi, ya_lo = (
            sem(n) for n in ("conv_mean", "conv_centered", "conv_sq", "conv_var", "conv_root", "conv_norm",
                             "conv_silu", "yc_hi", "yc_lo", "ya_hi", "ya_lo"))
        lam_dot, lam_exp, lam_ready, bias_masked = sem("lam_dot"), sem("lam_exp"), sem("lam_ready"), sem("bias_masked")
        dve_link, act_link, pool_link = sem("dve_link"), sem("act_link"), sem("pool_link")

        def linker(eng, link_sem):
            count = [0]

            def link(ins):
                count[0] += 1
                ins.then_inc(link_sem, 1)
                eng.wait_ge(link_sem, count[0])
            return link

        def row_bcast(ap, n):
            return bass.AP(ap.tensor, ap.offset, [[0, P], [1, n]])

        def items(kind):
            todo = list(plan(kind))
            for i, item in enumerate(todo):
                yield item, i + 1 < len(todo) and todo[i + 1][0] == "step"

        def b_bank(n):
            return ps[:, n % 2, :]

        def score_bank(kind, u, part):
            return ps[:, 4 + (part if kind == "diff" else u % 2), :]

        PT_BANK, OUT_BANK = 6, 7

        NORM_LAST = [C_CROSS - 1, C_RELU - 1, C_LAYER - 1]
        for layer in range(2):
            f1, c_att, f2 = c_layer(layer)
            NORM_LAST += [c_att - 1, f2 - 1, f2 + 3 * GLU_BLOCKS - 1]
        N_NORMS = len(NORM_LAST)
        half = {3: 0.5, 5: 0.5, 6: 0.5, 8: 0.5}
        post_gains = [w["post_mix_g"][0], w["post_x_g"][0], w["post_ffn_g"][0]] + [
            w["norm_g_2"][layer, j] for layer in range(2) for j in (1, 3, 5)]
        pre_gains = [w["pre_mix_g"][0], w["mem_g"][0], w["pre_x_g"][0], w["pre_ffn_g"][0]] + [
            w["norm_g_2"][layer, j] for layer in range(2) for j in (0, 2, 4)]

        def wcols(m, c0, n, k0=0, kn=KT):
            return m[k0 * P:(k0 + kn) * P, c0:c0 + n].rearrange("(k p) n -> p k n", p=P)

        block = ctx.enter_context(nc.Block())

        @block.sync
        def _(sp):
            def load(c, src, dims=KT):
                slot = c % NSLOT if isinstance(c, int) else None
                if c >= NSLOT:
                    sp.wait_ge(lo_done, c - NSLOT + 1)
                sp.dma_start(raw[:, slot, :].rearrange("p (k n) -> p k n", k=dims), src).then_inc(landed[slot], 16)

            def load_in_loop(c0, i, per, j, src, dims=KT):
                slot = (c0 + j) % NSLOT
                sp.wait_ge(lo_done, i * per + (c0 + j - NSLOT + 1))
                sp.dma_start(raw[:, slot, :].rearrange("p (k n) -> p k n", k=dims), src).then_inc(landed[slot], 16)

            def load_pre_gain(n):
                if n:
                    sp.wait_ge(normed, TT * n)
                sp.dma_start(gain[:, 1, :], row_bcast(pre_gains[n], D)).then_inc(gains_in[1], 16)

            def load_gains(j):
                if j:
                    sp.wait_ge(t1_post, TT * j)
                sp.dma_start(gain[:, 0, :], row_bcast(post_gains[j], D)).then_inc(gains_in[0], 16)
                if j < N_NORMS - 1:
                    load_pre_gain(2 + j)

            def load_stage(kind, sources, norm):
                for name, digit, c, _ in plan(kind):
                    if c is None:
                        continue
                    if c == 2:
                        load_small()
                    m, at = sources[name]
                    if name == "o":
                        load(c, m[256 * digit:256 * digit + 256, :].rearrange("(k p) n -> p k n", p=P), 2)
                    else:
                        load(c, wcols(m, at + 256 * digit, 256))
                load_gains(norm)

            def load_small():
                sp.dma_start(tab[:, P:TABLE_COLS], table[:, P:TABLE_COLS]).then_inc(tab_in, 16)
                load_pre_gain(1)
                sp.dma_start(mem_rows, w["mem"][0].rearrange("(t p) d -> p t d", p=P)).then_inc(mem_in, 16)
                small = [
                    (ws_raw, w["w_s"][0].rearrange("h t s -> t h s")),
                    (par_rows[0:62, :], w["w_dw"][0].rearrange("k (i p) -> (k i) p", p=P)),
                    (par_rows[62:64, :], w["b_dw"][0].rearrange("(i p) -> i p", p=P)),
                    (par_rows[64:66, :], w["conv_gn_g"][0].rearrange("(i p) -> i p", p=P)),
                    (par_rows[66:68, :], w["conv_gn_b"][0].rearrange("(i p) -> i p", p=P)),
                    (sub_gain[:, :], row_bcast(w["diff_subln_2"][0], P)),
                    (ln_g, row_bcast(w["gate_ln_g"][0], 256)),
                    (ln_b, row_bcast(w["gate_ln_b"][0], 256)),
                    (lam_rows[:, :, :].rearrange("p a b -> p (a b)"), row_bcast(w["diff_lambda_2"][0, 0], 256)),
                    (dist, table[:, TABLE_COLS:TABLE_COLS + 512])]
                bs = w["b_s"][0]
                for odd in range(2):
                    for c in range(TT):
                        small.append((b_mix[64 * odd:64 * odd + 64, :, c * P:(c + 1) * P],
                                      bass.AP(bs.tensor, bs.offset + odd * P, [[0, 64], [2 * P, 2], [1, P]])))
                assert len(small) == N_SMALL
                for dst, src in small:
                    sp.dma_start(dst, src).then_inc(small_in, 16)

            for t in range(TT):
                sp.dma_start(x[:, t, :], w["x"][0, t * P:(t + 1) * P, :]).then_inc(x_in, 16)
            sp.dma_start(ident, table[:, 0:P]).then_inc(tab_in, 16)
            load_pre_gain(0)
            w_in, w_xkv = w["w_in"][0], w["w_xkv"][0]
            load_stage("moba", dict(g=(w_in, 2304), a=(w_in, 2048), u=(w_in, 0), w=(w_in, 256), q=(w_in, 512),
                                    k=(w_in, 1024), v=(w_in, 1536), K=(w_xkv, 0), V=(w_xkv, D),
                                    o=(w["w_out"][0], 0)), 0)
            load_stage("cross", dict(q=(w["w_xq"][0], 0), o=(w["w_xo"][0], 0)), 1)

            up, down = w["w_ff1"][0], w["w_ff2"][0]
            load(C_RELU, wcols(up, 0, 256))
            with sp.Fori(0, (RELU_BLOCKS - 1) // 3) as i:
                for j in range(3):
                    load_in_loop(C_RELU + 1, i, 6, 2 * j,
                                 up[:, bass.ds(i * 768 + (256 * j + 256), 256)].rearrange("(k p) n -> p k n", p=P))
                    load_in_loop(C_RELU + 1, i, 6, 2 * j + 1,
                                 down[bass.ds(i * 768 + 256 * j, 256), :].rearrange("(k p) n -> p k n", p=P), 2)
            load(C_LAYER - 1, down[FF1 - 256:FF1, :].rearrange("(k p) n -> p k n", p=P), 2)
            load_gains(2)

            def gated(c0, which, layer, j):
                wg, wu, wd = (w[f"{which}_{n}_2"][layer] for n in ("wg", "wu", "wd"))
                load(c0, wcols(wg, 0, 256))
                load(c0 + 1, wcols(wu, 0, 256))
                with sp.Fori(0, GLU_BLOCKS - 1) as i:
                    load_in_loop(c0 + 2, i, 3, 0, wg[:, bass.ds(i * 256 + 256, 256)].rearrange("(k p) n -> p k n", p=P))
                    load_in_loop(c0 + 2, i, 3, 1, wu[:, bass.ds(i * 256 + 256, 256)].rearrange("(k p) n -> p k n", p=P))
                    load_in_loop(c0 + 2, i, 3, 2, wd[bass.ds(i * 256, 256), :].rearrange("(k p) n -> p k n", p=P), 2)
                load(c0 + 3 * GLU_BLOCKS - 1, wd[FF2 - 256:FF2, :].rearrange("(k p) n -> p k n", p=P), 2)
                load_gains(j)

            for layer, (kind, m_in, m_out) in enumerate((("diff", "diff_w_in_2", "diff_w_out_2"),
                                                         ("near", "na_w_in_2", "na_w_out_2"))):
                f1, c_att, f2 = c_layer(layer)
                gated(f1, "ffn1", layer, 3 + 3 * layer)
                m = w[m_in][0]
                load_stage(kind, dict(q=(m, 0), k=(m, D), v=(m, 2 * D), o=(w[m_out][0], 0)), 4 + 3 * layer)
                gated(f2, "ffn2", layer, 5 + 3 * layer)
            for t in range(TT):
                sp.wait_ge(x_new, TT * (N_NORMS - 1) + t + 1)
                sp.dma_start(out[0, t * P:(t + 1) * P, :], x[:, t, :]).then_inc(out_done, 16)
            sp.wait_ge(out_done, 16 * TT)

        @block.gpsimd
        def _(pool):
            link = linker(pool, pool_link)
            pool.memset(minus_half[:, :], -0.5).then_inc(const_set, 1)
            pool.memset(eps_col[:, :], EPS).then_inc(const_set, 1)
            pool.memset(conv_in[:, :, 0:30], 0.0).then_inc(const_set, 1)
            def load_bias(p0, n):
                pool.wait_ge(o_lo, ATT["diff"]["e0"])
                rpb = w["na_rpb_2"]
                for p in range(p0, p0 + n):
                    r, c = p // 64, p % 64
                    pool.dma_start(bias[p:p + 1], bass.AP(rpb.tensor, (5 - r) * 31 + 15 - c, [[465, 16], [31, 6], [1, 64]])
                                 ).then_inc(bias_in, 16)

            def inverse_root(dst, src, ready, count, done):
                pool.wait_ge(ready, count)
                link(pool.tensor_scalar(dst, src, EPS, None, ALU.add))
                pool.tensor_tensor(dst, dst, minus_half[:, 0:1], ALU.pow).then_inc(done, 1)

            def pre_norm(n):
                for t in range(TT):
                    k = TT * n + t
                    inverse_root(rstd[:, k:k + 1], ssq[:, k:k + 1], sq_pre, k + 1, r_pre)

            def norm(j):
                for t in range(TT):
                    k = 32 + TT * j + t
                    inverse_root(rstd[:, k:k + 1], ssq[:, k:k + 1], sq_post, TT * j + t + 1, r_post)
                if j < N_NORMS - 1:
                    pre_norm(2 + j)

            pool.wait_ge(const_set, 1)
            pre_norm(0)
            pre_norm(1)
            pool.wait_ge(small_in, 16 * N_SMALL)
            pool.affine_select(out=ws_raw, in_=ws_raw, compare_op=ALU.is_ge, fill=0.0, base=0,
                               pattern=[[0, 4], [-1, P]], channel_multiplier=1).then_inc(masked, 1)
            for t in range(TT):
                inverse_root(ln_s[:, 6 + t:7 + t], ln_s[:, 4 + t:5 + t], v_sq, t + 1, v_r)
            norm(0)
            norm(1)
            load_bias(0, 64)
            norm(2)
            load_bias(64, 64)
            pool.wait_ge(bias_in, 16 * P)
            for h in range(16):
                pool.tensor_tensor(bias[:, h], bias[:, h],
                                   window.rearrange("p (j c) -> p j c", j=1).broadcast_to([P, 6, 64]),
                                   ALU.add).then_inc(bias_masked, 1)
            norm(3)
            for u in range(8):
                pool.wait_ge(sub_sq_done, TT * (u + 1))
                link(pool.tensor_scalar(sub_stat[:, u % 2, 2:4], sub_stat[:, u % 2, 0:2], EPS, None, ALU.add))
                pool.tensor_tensor(sub_stat[:, u % 2, 2:4], sub_stat[:, u % 2, 2:4], minus_half[:, :],
                                   ALU.pow).then_inc(sub_r, 1)
            for j in range(4, N_NORMS):
                norm(j)

        @block.scalar
        def _(act):
            link = linker(act, act_link)

            def split(c):
                if c >= N_CHUNKS:
                    return
                slot = c % NSLOT
                act.wait_ge(landed[slot], 16 * (c // NSLOT + 1))
                if c >= NSLOT:
                    act.wait_ge(used, c - NSLOT + 1)
                act.copy(w_hi[:, slot, :], raw[:, slot, :]).then_inc(hi_done, 1)

            def split_in_loop(c, i, per):
                if isinstance(i, int):
                    return split(c + i * per)
                slot = c % NSLOT
                act.wait_ge(landed[slot], i * (16 * per // NSLOT) + 16 * (c // NSLOT + 1))
                act.wait_ge(used, i * per + (c - NSLOT + 1))
                act.copy(w_hi[:, slot, :], raw[:, slot, :]).then_inc(hi_done, 1)

            def squares(n, src, src_ready):
                for t in range(TT):
                    src_ready(t)
                    k = TT * n + t
                    if n == 0:
                        dump = t1[:, t, :]
                    elif n == 1:
                        dump = big[:, t * D:(t + 1) * D]
                    else:
                        dump = ps[:, 2 * t:2 * t + 2, :].rearrange("p a b -> p (a b)")
                    act.activation(dump, src[:, t, :], ACT.Square, scale=1.0 / 32,
                                   accum_out=ssq[:, k:k + 1]).then_inc(sq_pre, 1)

            def turned_hi(n, dst, bank=4):
                for b in range(4):
                    t, k0 = b // 2, 4 * (b % 2)
                    act.wait_ge(turned, 4 * n + b + 1)
                    act.copy(dst[0][:, k0:k0 + 4, t * P:(t + 1) * P],
                             ps[:, bank + b, :].rearrange("p (k s) -> p k s", k=4)).then_inc(h_hi, 1)

            def norm(j):
                for t in range(TT):
                    if t == 0:
                        act.wait_ge(y_half, j + 1)
                    else:
                        act.wait_ge(used, NORM_LAST[j] + 1)
                    k = 32 + TT * j + t
                    act.activation(t1[:, t, :], ps[:, 2 * t:2 * t + 2, :].rearrange("p a b -> p (a b)"), ACT.Square,
                                   scale=1.0 / 32, accum_out=ssq[:, k:k + 1]).then_inc(sq_post, 1)
                if j < N_NORMS - 1:
                    squares(2 + j, x, lambda t: act.wait_ge(x_new, TT * j + t + 1))
                    turned_hi(2 + j, hT)
                    split(NORM_LAST[j] + NSLOT)

            def attention_step(kind, s):
                a = ATT[kind]
                n_units, u0, per, parts = a["units"], a["u0"], a["per_out"], a["parts"]
                if kind == "diff" and s >= 3:
                    u = s - 3
                    act.wait_ge(sub_turned, u + 1)
                    act.copy(yT[0][:, u, :], ps[:, OUT_BANK, 256:512]).then_inc(o_hi, 1)
                if s < n_units:
                    b = s % 2
                    act.wait_ge(m_ready, u0 + s + 1)
                    if s >= 2:
                        act.wait_ge(p_ready, u0 + s - 1)
                    for j in range(2 * parts):
                        if kind in ("moba", "near"):
                            src = att_bias[:, b, 256 * j:256 * j + 256]
                        else:
                            src = score_bank(kind, s, j // 2)[:, 256 * (j % 2):256 * (j % 2) + 256]
                        ins = act.activation(expd[:, b, 256 * j:256 * j + 256], src, ACT.Exp,
                                             bias=neg_top[:, b, j:j + 1], scale=1.0 if kind == "near" else a["scale"],
                                             accum_out=denom[:, b, j:j + 1])
                    ins.then_inc(e_ready, 1)
                if 0 <= s - 1 < n_units:
                    u = s - 1
                    act.wait_ge(t_ready, u0 + u + 1)
                    if u >= 2:
                        act.wait_ge(o_ready, u0 + u - 1)
                    act.copy(probT[:, u % 2, :], ps[:, PT_BANK, :]).then_inc(pt_ready, 1)
                if kind != "diff" and s >= 2 and (s - 2) % per == per - 1:
                    u = s - 2
                    act.wait_ge(o_ready, u0 + u + 1)
                    if kind == "cross":
                        act.copy(yT[0][:, 2 * u:2 * u + 2, :],
                                 ps[:, OUT_BANK, :].rearrange("p (a s) -> p a s", a=2)).then_inc(o_hi, 1)
                    else:
                        act.copy(yT[0][:, (2 if kind == "moba" else 0) + u // 2, :],
                                 ps[:, OUT_BANK, 0:256]).then_inc(o_hi, 1)
                if kind == "diff" and 0 <= s - 2 < n_units:
                    u = s - 2
                    act.wait_ge(o_ready, u0 + u + 1)
                    if u >= 2:
                        act.wait_ge(sub_on, u - 1)
                    for t in range(TT):
                        if u or t:
                            act.wait_ge(sub_sq_done, TT * u + t)
                        act.activation(sub_dump[:, 0, 0:P], ps[:, OUT_BANK, t * P:(t + 1) * P], ACT.Square,
                                       scale=P ** -0.5, accum_out=sub_stat[:, u % 2, t:t + 1]
                                       ).then_inc(sub_sq_done, 1)

            def other_step(name):
                if name == "mem":
                    turned_hi(1, yT)
                if name == "conv_var":
                    act.wait_ge(c_centered, 1)
                    act.activation(glu_a, sig, ACT.Square).then_inc(c_sq, 1)
                if name == "conv_root":
                    act.wait_ge(c_var, 1)
                    act.wait_ge(const_set, 2)
                    act.activation(glu_a, ps[:, 3, :], ACT.Sqrt, bias=eps_col[:, 0:1]).then_inc(c_root, 1)
                if name == "conv_out":
                    act.wait_ge(c_norm, 1)
                    for i in range(2):
                        act.activation(glu_a[:, 256 * i:256 * i + 256], sig[:, 256 * i:256 * i + 256], ACT.Silu,
                                       scale=par[:, 64 + i:65 + i], bias=par[:, 66 + i:67 + i]).then_inc(c_silu, 1)
                    act.wait_ge(c_silu, 2)
                    act.copy(yT[0][:, 6:8, :], glu_a.rearrange("p (a s) -> p a s", a=2)).then_inc(yc_hi, 1)
                if name == "gate_norm":
                    for t in range(TT):
                        act.wait_ge(v_centered, t + 1)
                        act.activation(prob[:, t, 0:256], va[:, t, :], ACT.Square, scale=1.0 / 16,
                                       accum_out=ln_s[:, 4 + t:5 + t]).then_inc(v_sq, 1)
                if name == "mix_out":
                    act.wait_ge(ya_raw, 1)
                    act.copy(yT[0][:, 0:2, :], gated_u.rearrange("p (a s) -> p a s", a=2)).then_inc(ya_hi, 1)
                if name == "lambda":
                    act.wait_ge(lam_dot, 2)
                    act.activation(lam[:, 2:4], lam[:, 0:2], ACT.Exp).then_inc(lam_exp, 1)

            def product_out(kind, name, digit, n):
                bank = b_bank(n)
                tiles = slice(2 * digit, 2 * digit + 2)
                if name == "g":
                    ins = act.activation(sig, bank, ACT.Sigmoid)
                elif name == "a":
                    ins = act.copy(glu_a, bank)
                elif name == "u":
                    ins = act.activation(uT, bank, ACT.Gelu)
                elif name == "w":
                    link(act.activation(va[:, 0, :], bank[:, 0:256], ACT.Gelu, accum_out=ln_s[:, 0:1]))
                    ins = act.activation(va[:, 1, :], bank[:, 256:512], ACT.Gelu, accum_out=ln_s[:, 1:2])
                elif name in "vV":
                    dst = vv if name == "v" else vm
                    ins = act.copy(dst[:, :, 256 * digit:256 * digit + 256], bank.rearrange("p (t d) -> p t d", t=TT))
                else:
                    dst = {"q": qT, "k": kT, "K": kmT}[name]
                    ins = act.copy(dst[:, tiles, :], bank.rearrange("p (a s) -> p a s", a=2))
                ins.then_inc(b_evac, 1)

            def stage(kind):
                for name, digit, c, n in plan(kind):
                    if name == "step":
                        attention_step(kind, digit)
                    elif c is None:
                        other_step(name)
                    else:
                        if name != "o":
                            act.wait_ge(used, c + 1)
                            product_out(kind, name, digit, n)
                        if c not in NORM_LAST:
                            split(c + NSLOT)

            squares(0, x, lambda t: act.wait_ge(x_in, 16 * TT))
            turned_hi(0, hT)
            split(0)
            split(1)
            squares(1, mem_rows, lambda t: act.wait_ge(mem_in, 16))
            split(2)
            stage("moba")
            norm(0)
            stage("cross")
            norm(1)

            act.wait_ge(used, C_RELU + 1)
            act.activation(gate, ps[:, 4, :], ACT.Relu).then_inc(gate_done, 1)
            split(C_RELU + NSLOT)
            act.wait_ge(hraw_done, 1)
            act.copy(hid[0][:, :, :], hraw.rearrange("p (a s) -> p a s", a=2)).then_inc(hid_hi, 1)
            with act.Fori(0, (RELU_BLOCKS - 1) // 3) as i:
                for j in range(3):
                    c0 = C_RELU + 1
                    act.wait_ge(used, i * 6 + (c0 + 2 * j + 1))
                    act.wait_ge(hraw_done, i * 3 + (j + 1))
                    act.activation(gate, ps[:, 4, :], ACT.Relu).then_inc(gate_done, 1)
                    split_in_loop(c0 + NSLOT + 2 * j, i, 6)
                    act.wait_ge(used, i * 6 + (c0 + 2 * j + 2))
                    act.wait_ge(hraw_done, i * 3 + (j + 2))
                    act.copy(hid[0][:, :, :], hraw.rearrange("p (a s) -> p a s", a=2)).then_inc(hid_hi, 1)
                    split_in_loop(c0 + NSLOT + 2 * j + 1, i, 6)
            norm(2)

            def gated(c0, f):
                b0 = RELU_BLOCKS + GLU_BLOCKS * f
                act.wait_ge(used, c0 + 1)
                act.activation(gate, ps[:, 4, :], ACT.Silu).then_inc(gate_done, 1)
                split(c0 + NSLOT)
                split(c0 + 1 + NSLOT)
                act.wait_ge(hraw_done, b0 + 1)
                act.copy(hid[0][:, :, :], hraw.rearrange("p (a s) -> p a s", a=2)).then_inc(hid_hi, 1)

                def step(i):
                    c = c0 + 2
                    act.wait_ge(used, i * 3 + (c + 1))
                    act.wait_ge(hraw_done, i + (b0 + 1))
                    act.activation(gate, ps[:, 4, :], ACT.Silu).then_inc(gate_done, 1)
                    split_in_loop(c + NSLOT, i, 3)
                    split_in_loop(c + NSLOT + 1, i, 3)
                    act.wait_ge(used, i * 3 + (c + 3))
                    act.wait_ge(hraw_done, i + (b0 + 2))
                    act.copy(hid[0][:, :, :], hraw.rearrange("p (a s) -> p a s", a=2)).then_inc(hid_hi, 1)
                    split_in_loop(c + NSLOT + 2, i, 3)

                with act.Fori(0, GLU_BLOCKS - 2) as i:
                    step(i)
                step(GLU_BLOCKS - 2)

            for layer, kind in enumerate(("diff", "near")):
                f1, c_att, f2 = c_layer(layer)
                gated(f1, 2 * layer)
                norm(3 + 3 * layer)
                stage(kind)
                norm(4 + 3 * layer)
                gated(f2, 2 * layer + 1)
                norm(5 + 3 * layer)

        @block.vector
        def _(dve):
            link = linker(dve, dve_link)

            def split(c):
                if c >= N_CHUNKS:
                    return
                slot = c % NSLOT
                dve.wait_ge(hi_done, c + 1)
                dve.tensor_tensor(w_lo[:, slot, :], raw[:, slot, :], w_hi[:, slot, :],
                                  ALU.subtract).then_inc(lo_done, 1)

            def split_in_loop(c, i, per):
                if isinstance(i, int):
                    return split(c + i * per)
                slot = c % NSLOT
                dve.wait_ge(hi_done, i * per + (c + 1))
                dve.tensor_tensor(w_lo[:, slot, :], raw[:, slot, :], w_hi[:, slot, :],
                                  ALU.subtract).then_inc(lo_done, 1)

            def scale_rows(n, src, dst):
                for t in range(TT):
                    k = TT * n + t
                    dve.wait_ge(r_pre, k + 1)
                    if t == 0:
                        dve.wait_ge(gains_in[1], 16 * (n + 1))
                    dve.scalar_tensor_tensor(dst[:, t, :], src[:, t, :], rstd[:, k:k + 1], gain[:, 1, :],
                                             ALU.mult, ALU.mult).then_inc(normed, 1)

            def turned_lo(n, dst, bank=4):
                for b in range(4):
                    t, k0 = b // 2, 4 * (b % 2)
                    dve.wait_ge(h_hi, 4 * n + b + 1)
                    part = (slice(None), slice(k0, k0 + 4), slice(t * P, (t + 1) * P))
                    dve.tensor_tensor(dst[1][part], ps[:, bank + b, :].rearrange("p (k s) -> p k s", k=4),
                                      dst[0][part], ALU.subtract).then_inc(h_lo, 1)

            def norm(j):
                for t in range(TT):
                    k = 32 + TT * j + t
                    dve.wait_ge(r_post, TT * j + t + 1)
                    if t == 0:
                        dve.wait_ge(gains_in[0], 16 * (j + 1))
                    dve.scalar_tensor_tensor(t1[:, t, :], ps[:, 2 * t:2 * t + 2, :].rearrange("p a b -> p (a b)"),
                                             rstd[:, k:k + 1], gain[:, 0, :], ALU.mult, ALU.mult).then_inc(t1_post, 1)
                    dve.wait_ge(t1_post, TT * j + t + 1)
                    dve.scalar_tensor_tensor(x[:, t, :], t1[:, t, :], half.get(j, 1.0), x[:, t, :],
                                             ALU.mult, ALU.add).then_inc(x_new, 1)
                if j < N_NORMS - 1:
                    scale_rows(2 + j, x, t1)
                    turned_lo(2 + j, hT)
                    split(NORM_LAST[j] + NSLOT)

            scale_rows(0, x, t1)
            turned_lo(0, hT)
            split(0)
            split(1)
            scale_rows(1, mem_rows, mem_rows)
            split(2)

            def conv_taps(k0, k1):
                for k in range(k0, k1):
                    for i in range(2):
                        acc = sig[:, 256 * i:256 * i + 256]
                        tap = par[:, 2 * k + i:2 * k + i + 1]
                        if k == 0:
                            dve.tensor_scalar(acc, conv_in[:, i, 0:S], tap, par[:, 62 + i:63 + i],
                                              ALU.mult, ALU.add).then_inc(conv_done, 1)
                        else:
                            dve.wait_ge(conv_done, 2 * (k - 1) + i + 1)
                            dve.scalar_tensor_tensor(acc, conv_in[:, i, k:k + S], tap, acc,
                                                     ALU.mult, ALU.add).then_inc(conv_done, 1)

            def other_step(name, digit):
                if name == "mem":
                    turned_lo(1, yT)
                if name == "consts":
                    dve.wait_ge(par_T, 1)
                    dve.tensor_copy(par[:, :], ps[:, 2, 0:68]).then_inc(par_ready, 1)
                    dve.wait_ge(par_T, 2)
                    dve.tensor_copy(wsT, ps[:, 3, :].rearrange("p (h t) -> p h t", h=4)).then_inc(par_ready, 1)
                    dve.wait_ge(small_in, 16 * N_SMALL)
                    dve.tensor_scalar(sub_gain[:, :], sub_gain[:, :], 1.0 - LAM_INIT, None, ALU.mult)
                    dve.wait_ge(par_ready, 2)
                if name == "glu":
                    dve.wait_ge(b_evac, 2)
                    dve.wait_ge(const_set, 3)
                    dve.tensor_tensor(conv_in[:, :, 30:30 + S], glu_a.rearrange("p (i s) -> p i s", i=2),
                                      sig.rearrange("p (i s) -> p i s", i=2), ALU.mult).then_inc(glu_ready, 1)
                    dve.wait_ge(glu_ready, 1)
                if name == "taps":
                    conv_taps(4 * digit, min(4 * digit + 4, 31))
                if name == "conv_mean":
                    dve.wait_ge(cm_ready, 1)
                    dve.tensor_tensor(sig, sig, ps[:, 2, :], ALU.subtract).then_inc(c_centered, 1)
                if name == "conv_root":
                    dve.wait_ge(c_root, 1)
                    link(dve.reciprocal(glu_a, glu_a))
                    dve.tensor_tensor(sig, sig, glu_a, ALU.mult).then_inc(c_norm, 1)
                if name == "conv_out":
                    dve.wait_ge(yc_hi, 1)
                    dve.tensor_tensor(yT[1][:, 6:8, :], glu_a.rearrange("p (a s) -> p a s", a=2), yT[0][:, 6:8, :],
                                      ALU.subtract).then_inc(yc_lo, 1)
                if name == "gate_norm":
                    dve.wait_ge(b_evac, product_number("moba", "w", 0) + 1)
                    link(dve.tensor_scalar(ln_s[:, 2:4], ln_s[:, 0:2], 1.0 / 256, None, ALU.mult))
                    for t in range(TT):
                        dve.tensor_scalar(va[:, t, :], va[:, t, :], ln_s[:, 2 + t:3 + t], None,
                                          ALU.subtract).then_inc(v_centered, 1)
                if name == "gate_scale":
                    for t in range(TT):
                        dve.wait_ge(v_r, t + 1)
                        link(dve.scalar_tensor_tensor(va[:, t, :], va[:, t, :], ln_s[:, 6 + t:7 + t], ln_g,
                                                      ALU.mult, ALU.mult))
                        dve.tensor_tensor(va[:, t, :], va[:, t, :], ln_b, ALU.add).then_inc(v_normed, 1)
                if name == "mix_raw":
                    dve.wait_ge(mix_ready, 1)
                    link(dve.tensor_tensor(rope_t[:, :], ps[:, 2, :], b_mix.rearrange("p a s -> p (a s)"), ALU.add))
                    dve.tensor_tensor(gated_u, rope_t[:, :], uT, ALU.mult).then_inc(ya_raw, 1)
                if name == "mix_out":
                    dve.wait_ge(ya_hi, 1)
                    dve.tensor_tensor(yT[1][:, 0:2, :], gated_u.rearrange("p (a s) -> p a s", a=2),
                                      yT[0][:, 0:2, :], ALU.subtract).then_inc(ya_lo, 1)
                    dve.wait_ge(ya_lo, 1)
                if name == "lambda":
                    for j in range(2):
                        dve.tensor_tensor_reduce(sub_out[:, j, 0:64], lam_rows[:, 2 * j, :],
                                                 lam_rows[:, 2 * j + 1, :], 1.0, 0.0, ALU.mult, ALU.add,
                                                 lam[:, j:j + 1]).then_inc(lam_dot, 1)
                    dve.wait_ge(lam_exp, 1)
                    link(dve.tensor_tensor(lam[:, 5:6], lam[:, 3:4], lam[:, 2:3], ALU.subtract))
                    link(dve.tensor_scalar(lam[:, 4:5], lam[:, 5:6], LAM_INIT, None, ALU.subtract))
                if name == "rot":
                    rope(digit)

            def attention_step(kind, s, done_before, chunk_next):
                a = ATT[kind]
                n_units, u0, per, parts = a["units"], a["u0"], a["per_out"], a["parts"]
                n = 2 * parts

                def scores_max(s):
                    b = s % 2
                    dve.wait_ge(s_ready, u0 + s + 1)
                    if s >= 2:
                        dve.wait_ge(e_ready, u0 + s - 1)
                    if kind == "moba":
                        slope = 2.0 ** -(s + 1)
                        link(dve.scalar_tensor_tensor(att_bias[:, b, :], dist, -slope / a["scale"],
                                                      score_bank(kind, s, 0),
                                                      ALU.mult, ALU.add))
                        src = att_bias[:, b, :].rearrange("p (j s) -> p j s", j=n)
                    elif kind == "near":
                        if s == 0:
                            dve.wait_ge(bias_masked, 16)
                        for t in range(TT):
                            ins = dve.scalar_tensor_tensor(
                                att_bias[:, b, 256 * t:256 * t + 256].rearrange("p (j c) -> p j c", j=4),
                                score_bank(kind, s, 0)[:, 256 * t:256 * t + 256].rearrange("p (j c) -> p j c", j=4),
                                a["scale"],
                                bias[:, s, 2 - 2 * t:6 - 2 * t, :], ALU.mult, ALU.add)
                        link(ins)
                        src = att_bias[:, b, :].rearrange("p (j s) -> p j s", j=n)
                    elif parts == 2:
                        src = ps[:, 4:6, :].rearrange("p a (j s) -> p (a j) s", j=2)
                    else:
                        src = score_bank(kind, s, 0).rearrange("p (j s) -> p j s", j=n)
                    link(dve.tensor_reduce(top[:, b, 0:n], src, AX_X, ALU.max))
                    dve.tensor_scalar(neg_top[:, b, 0:n], top[:, b, 0:n],
                                      -1.0 if kind == "near" else -a["scale"], None, ALU.mult).then_inc(m_ready, 1)

                def normalise(u):
                    b = u % 2
                    dve.wait_ge(e_ready, u0 + u + 1)
                    link(dve.reciprocal(inv_denom[:, b, 0:n], denom[:, b, 0:n]))
                    if u >= 2:
                        dve.wait_ge(t_ready, u0 + u - 1)
                    if parts == 2:
                        link(dve.tensor_scalar(inv_denom[:, b, 2:4], inv_denom[:, b, 2:4], lam[:, 4:5], None, ALU.mult))
                    for t in range(TT):
                        ins = dve.tensor_scalar(prob[:, b, 256 * t:256 * t + 256], expd[:, b, 256 * t:256 * t + 256],
                                                inv_denom[:, b, t:t + 1], None, ALU.mult)
                    if parts == 2:
                        link(ins)
                        for t in range(TT):
                            dst = prob[:, b, 256 * t:256 * t + 256]
                            ins = dve.scalar_tensor_tensor(dst, expd[:, b, 512 + 256 * t:768 + 256 * t],
                                                           inv_denom[:, b, 2 + t:3 + t], dst, ALU.mult, ALU.add)
                    ins.then_inc(p_ready, 1)

                def sub_norm(u):
                    dve.wait_ge(sub_r, u + 1)
                    if u >= 2:
                        dve.wait_ge(sub_turned, u - 1)
                    for t in range(TT):
                        ins = dve.scalar_tensor_tensor(sub_out[:, u % 2, t * P:(t + 1) * P],
                                                       ps[:, OUT_BANK, t * P:(t + 1) * P],
                                                       sub_stat[:, u % 2, 2 + t:3 + t], sub_gain[:, :],
                                                       ALU.mult, ALU.mult)
                    ins.then_inc(sub_on, 1)

                def out_lo(u):
                    if u % per != per - 1:
                        return
                    e = u // per
                    dve.wait_ge(o_hi, a["e0"] + e + 1)
                    bank = ps[:, OUT_BANK, :]
                    if kind == "diff":
                        tiles, src = slice(u, u + 1), bank[:, 256:512].rearrange("p (a s) -> p a s", a=1)
                    elif kind == "cross":
                        tiles, src = slice(2 * u, 2 * u + 2), bank.rearrange("p (a s) -> p a s", a=2)
                    else:
                        tile = (2 if kind == "moba" else 0) + e
                        tiles, src = slice(tile, tile + 1), bank[:, 0:256].rearrange("p (a s) -> p a s", a=1)
                    dve.tensor_tensor(yT[1][:, tiles, :], src, yT[0][:, tiles, :], ALU.subtract).then_inc(o_lo, 1)

                if s < n_units:
                    scores_max(s)
                if kind == "diff" and s >= 3:
                    out_lo(s - 3)
                elif s >= 3 and not done_before:
                    out_lo(s - 3)
                if 0 <= s - 1 < n_units and not done_before:
                    normalise(s - 1)
                if s < n_units and chunk_next:
                    normalise(s)
                if kind == "diff" and 0 <= s - 2 < n_units:
                    sub_norm(s - 2)
                if kind != "diff" and s >= 2 and chunk_next:
                    out_lo(s - 2)

            def stage(kind):
                late, done_before = None, False
                for (name, digit, c, n), step_next in items(kind):
                    if name == "step":
                        attention_step(kind, digit, done_before, not step_next)
                        done_before = not step_next
                        if late is not None and not step_next:
                            split(late)
                            late = None
                    elif c is None:
                        other_step(name, digit)
                    elif step_next:
                        late = c + NSLOT
                    elif c not in NORM_LAST:
                        split(c + NSLOT)

            def hidden_lo(n):
                dve.wait_ge(hid_hi, n)
                dve.tensor_tensor(hid[1][:, :, :], hraw.rearrange("p (a s) -> p a s", a=2), hid[0][:, :, :],
                                  ALU.subtract).then_inc(hid_lo, 1)

            def rope(j):
                order = [d for name, d, _, _ in plan("diff") if name == "rot"].index(j)
                dst = (qT, kT)[j // 4][:, 2 * (j % 4):2 * (j % 4) + 2, :]
                sin2, cos2 = (m.rearrange("p (a s) -> p a s", a=1).broadcast_to([P, 2, S]) for m in (sin, cos))
                part = rope_t.rearrange("p (a s) -> p a s", a=2)
                dve.wait_ge(rot_ready, order + 1)
                if order:
                    dve.wait_ge(rope_done, order)
                dve.tensor_tensor(part, ps[:, 2 + order % 2, :].rearrange("p (a s) -> p a s", a=2), sin2,
                                  ALU.mult).then_inc(rope_mul, 1)
                link(dve.tensor_tensor(dst, dst, cos2, ALU.mult))
                dve.wait_ge(rope_mul, order + 1)
                dve.tensor_tensor(dst, dst, part, ALU.add).then_inc(rope_done, 1)

            stage("moba")
            norm(0)
            stage("cross")
            norm(1)

            dve.wait_ge(gate_done, 1)
            dve.scalar_tensor_tensor(hraw, ps[:, 4, :], 0.0, gate, ALU.max, ALU.mult).then_inc(hraw_done, 1)
            split(C_RELU + NSLOT)
            hidden_lo(1)
            with dve.Fori(0, (RELU_BLOCKS - 1) // 3) as i:
                for j in range(3):
                    c = C_RELU + 1 + 2 * j
                    dve.wait_ge(gate_done, i * 3 + (j + 2))
                    dve.wait_ge(hid_lo, i * 3 + (j + 1))
                    dve.scalar_tensor_tensor(hraw, ps[:, 4, :], 0.0, gate,
                                             ALU.max, ALU.mult).then_inc(hraw_done, 1)
                    split_in_loop(c + NSLOT, i, 6)
                    hidden_lo(i * 3 + (j + 2))
                    split_in_loop(c + 1 + NSLOT, i, 6)
            norm(2)

            def gated(c0, f):
                b0 = g0 = RELU_BLOCKS + GLU_BLOCKS * f
                split(c0 + NSLOT)
                dve.wait_ge(gate_done, g0 + 1)
                dve.wait_ge(used, c0 + 2)
                dve.tensor_tensor(hraw, gate, ps[:, 5, :], ALU.mult).then_inc(hraw_done, 1)
                split(c0 + 1 + NSLOT)
                hidden_lo(b0 + 1)

                def step(i):
                    c = c0 + 2
                    split_in_loop(c + NSLOT, i, 3)
                    dve.wait_ge(gate_done, i + (g0 + 2))
                    dve.wait_ge(used, i * 3 + (c + 2))
                    dve.wait_ge(hid_lo, i + (b0 + 1))
                    dve.tensor_tensor(hraw, gate, ps[:, 5, :], ALU.mult).then_inc(hraw_done, 1)
                    split_in_loop(c + NSLOT + 1, i, 3)
                    hidden_lo(i + (b0 + 2))
                    split_in_loop(c + NSLOT + 2, i, 3)

                with dve.Fori(0, GLU_BLOCKS - 2) as i:
                    step(i)
                step(GLU_BLOCKS - 2)

            for layer, kind in enumerate(("diff", "near")):
                f1, c_att, f2 = c_layer(layer)
                gated(f1, 2 * layer)
                norm(3 + 3 * layer)
                stage(kind)
                norm(4 + 3 * layer)
                gated(f2, 2 * layer + 1)
                norm(5 + 3 * layer)

        @block.tensor
        def _(pe):
            def transposed_product(src, slot, bank, norm=None):
                wh, wl = (m[:, slot, :].rearrange("p (k n) -> p k n", k=KT) for m in (w_hi, w_lo))
                for n in range(2):
                    o = bank[:, 256 * n:256 * n + 256]
                    for k in range(KT):
                        if norm is not None and n == 0 and k % 4 == 0:
                            pe.wait_ge(h_lo, 4 * norm + 3 + k // 4)
                        hi, lo = wh[:, k, 128 * n:128 * n + 128], wl[:, k, 128 * n:128 * n + 128]
                        pe.matmul(o, hi, src[0][:, k, :], start=(k == 0), stop=False)
                        pe.matmul(o, hi, src[1][:, k, :], start=False, stop=False)
                        ins = pe.matmul(o, lo, src[0][:, k, :], start=False, stop=(k == KT - 1))
                return ins

            def rows_product(src, tiles, slot, width, banks, first, last, half_sem=None):
                wh, wl = (m[:, slot, :].rearrange("p (k n) -> p k n", k=len(tiles)) for m in (w_hi, w_lo))
                for t in range(TT):
                    for nb in range(len(banks[t])):
                        o = banks[t][nb]
                        cols = slice(width * nb, width * nb + width)
                        for i, k in enumerate(tiles):
                            hi, lo = (m[:, k, t * P:(t + 1) * P] for m in src)
                            pe.matmul(o, hi, wh[:, i, cols], start=first and i == 0, stop=False)
                            pe.matmul(o, hi, wl[:, i, cols], start=False, stop=False)
                            ins = pe.matmul(o, lo, wh[:, i, cols], start=False, stop=last and i == len(tiles) - 1)
                    if t == 0 and half_sem is not None:
                        ins.then_inc(half_sem, 1)
                return ins

            def turn(n, src=t1, bank=4):
                for t in range(TT):
                    pe.wait_ge(normed, TT * n + t + 1)
                    for b in range(2):
                        for k in range(4):
                            col = P * (4 * b + k)
                            ins = pe.transpose(ps[:, bank + 2 * t + b, k * P:(k + 1) * P], src[:, t, col:col + P],
                                               ident)
                        ins.then_inc(turned, 1)

            def attention_step(kind, s):
                a = ATT[kind]
                n_units, u0, per, parts = a["units"], a["u0"], a["per_out"], a["parts"]

                def scores(s):
                    if s >= (1 if parts == 2 else 2):
                        pe.wait_ge(e_ready, u0 + s - (0 if parts == 2 else 1))
                    for part in range(parts):
                        for t in range(TT):
                            o = score_bank(kind, s, part)[:, 256 * t:256 * t + 256]
                            if kind == "cross":
                                for i in range(2):
                                    ins = pe.matmul(o, qT[:, 2 * s + i, t * P:(t + 1) * P], kmT[:, 2 * s + i, :],
                                                    start=(i == 0), stop=(i == 1))
                            else:
                                head = 2 * s + part if parts == 2 else s
                                rows = slice(64 * (head % 2), 64 * (head % 2) + 64)
                                ins = pe.matmul(o, qT[rows, head // 2, t * P:(t + 1) * P], kT[rows, head // 2, :],
                                                start=True, stop=True)
                    ins.then_inc(s_ready, 1)

                def turn_prob(u):
                    b = u % 2
                    pe.wait_ge(p_ready, u0 + u + 1)
                    if u >= 1:
                        pe.wait_ge(pt_ready, u0 + u)
                    for kt in range(TT):
                        for t in range(TT):
                            ins = pe.transpose(ps[:, PT_BANK, 256 * kt + t * P:256 * kt + (t + 1) * P],
                                               prob[:, b, 256 * t + kt * P:256 * t + (kt + 1) * P], ident)
                    ins.then_inc(t_ready, 1)

                def weigh_values(u):
                    b, e = u % 2, u // per
                    pe.wait_ge(pt_ready, u0 + u + 1)
                    bank = ps[:, OUT_BANK, :]
                    if kind == "diff":
                        if u:
                            pe.wait_ge(o_lo, a["e0"] + u)
                        for t in range(TT):
                            for kt in range(TT):
                                col = 256 * kt + t * P
                                ins = pe.matmul(bank[:, t * P:(t + 1) * P], probT[:, b, col:col + P],
                                                vv[:, kt, P * u:P * u + P], start=(kt == 0), stop=(kt == TT - 1))
                        ins.then_inc(o_ready, 1)
                        return
                    if e:
                        pe.wait_ge(o_lo, a["e0"] + e)
                    values = vm if kind == "cross" else vv
                    for et in range(2 if kind == "cross" else 1):
                        if kind == "cross":
                            o, cols = bank[:, 256 * et:256 * et + 256], slice(256 * u + P * et, 256 * u + P * et + P)
                        else:
                            o, cols = bank[64 * (u % 2):64 * (u % 2) + 64, 0:256], slice(64 * u, 64 * u + 64)
                        for kt in range(TT):
                            ins = pe.matmul(o, values[:, kt, cols], probT[:, b, 256 * kt:256 * kt + 256],
                                            start=(kt == 0), stop=(kt == TT - 1))
                    ins.then_inc(o_ready, 1)

                def turn_result(u):
                    pe.wait_ge(sub_on, u + 1)
                    for t in range(TT):
                        ins = pe.transpose(ps[:, OUT_BANK, 256 + t * P:256 + (t + 1) * P],
                                           sub_out[:, u % 2, t * P:(t + 1) * P], ident)
                    ins.then_inc(sub_turned, 1)

                if kind == "diff" and s >= 3:
                    turn_result(s - 3)
                if s < n_units:
                    if kind == "diff":
                        order = [d for name, d, _, _ in plan("diff") if name == "rot"]
                        pe.wait_ge(rope_done, 1 + max(order.index(s // 2), order.index(4 + s // 2)))
                    scores(s)
                if 0 <= s - 1 < n_units:
                    turn_prob(s - 1)
                if 0 <= s - 2 < n_units:
                    weigh_values(s - 2)

            def other_step(kind, name, digit, n_done):
                if name == "mem":
                    turn(1, mem_rows)
                    pe.wait_ge(tab_in, 32)
                if name == "consts":
                    pe.wait_ge(small_in, 16 * N_SMALL)
                    pe.transpose(ps[:, 2, 0:68], par_rows[:, :], ident[0:68, 0:68]).then_inc(par_T, 1)
                    pe.wait_ge(masked, 1)
                    for h in range(4):
                        ins = pe.transpose(ps[:, 3, h * P:(h + 1) * P], ws_raw[:, h, :], ident)
                    ins.then_inc(par_T, 1)
                if name == "conv_mean":
                    pe.wait_ge(ya_raw, 1)
                    pe.wait_ge(conv_done, 62)
                    pe.matmul(ps[:, 2, :], group_mean, sig, start=True, stop=True).then_inc(cm_ready, 1)
                if name == "conv_var":
                    pe.wait_ge(c_sq, 1)
                    pe.matmul(ps[:, 3, :], group_mean, glu_a, start=True, stop=True).then_inc(c_var, 1)
                if name == "mix":
                    pe.wait_ge(v_normed, TT)
                    for h in range(4):
                        for t in range(TT):
                            rows = slice(64 * (h % 2), 64 * (h % 2) + 64)
                            col = 256 * (h // 2) + t * P
                            ins = pe.matmul(ps[rows, 2, col:col + P], va[:, t, 64 * h:64 * h + 64], wsT[:, h, :],
                                            start=True, stop=True)
                    ins.then_inc(mix_ready, 1)
                if name == "rot":
                    order = [d for n, d, _, _ in plan("diff") if n == "rot"].index(digit)
                    chunk_n = [n for name, d, _, n in plan("diff") if name == "qk"[digit // 4] and d == digit % 4][0]
                    pe.wait_ge(b_evac, chunk_n + 1)
                    if order >= 2:
                        pe.wait_ge(rope_mul, order - 1)
                    for n in range(2):
                        ins = pe.matmul(ps[:, 2 + order % 2, 256 * n:256 * n + 256], rot,
                                        (qT, kT)[digit // 4][:, 2 * (digit % 4) + n, :], start=True, stop=True)
                    ins.then_inc(rot_ready, 1)

            def stage(kind, norm=None):
                outs = 0
                n_last = 0
                for name, digit, c, n in plan(kind):
                    if name == "step":
                        pe.wait_ge(b_evac, products_of(kind, digit))
                        attention_step(kind, digit)
                        continue
                    if c is None:
                        other_step(kind, name, digit, n_last)
                        continue
                    pe.wait_ge(lo_done, c + 1)
                    if name == "o":
                        out_product(kind, digit, c, outs, n_last)
                        outs += 1
                        continue
                    if n >= 2:
                        pe.wait_ge(b_evac, n - 1)
                    src = yT if name in "KV" else hT
                    if name in "wvV":
                        ins = rows_product(src, range(KT), c % NSLOT, 256,
                                           [[b_bank(n)[:, 256 * t:256 * t + 256]] for t in range(TT)], True, True)
                    else:
                        after = norm if c == STAGES[kind][0] else 1 if (name, digit) == ("K", 0) else None
                        ins = transposed_product(src, c % NSLOT, b_bank(n), after)
                    ins.then_inc(used, 1)
                    n_last = n

            def out_product(kind, digit, c, outs, n_last):
                if outs == 0:
                    pe.wait_ge(b_evac, n_last + 1)
                    if kind == "moba":
                        pe.wait_ge(c_root, 1)
                        pe.wait_ge(ya_lo, 1)
                    if kind == "diff":
                        pe.wait_ge(rope_mul, 8)
                if kind == "moba" and digit in (0, 3):
                    if digit == 3:
                        pe.wait_ge(yc_lo, 1)
                elif kind == "moba":
                    pe.wait_ge(o_lo, 2 * digit)
                elif kind == "cross":
                    pe.wait_ge(o_lo, ATT[kind]["e0"] + digit + 1)
                else:
                    pe.wait_ge(o_lo, ATT[kind]["e0"] + 2 * digit + 2)
                banks = [[ps[:, 2 * t + nb, :] for nb in range(2)] for t in range(TT)]
                rows_product(yT, range(2 * digit, 2 * digit + 2), c % NSLOT, 512, banks, outs == 0, outs == 3,
                             y_half if outs == 3 else None).then_inc(used, 1)

            pe.wait_ge(tab_in, 16)
            turn(0)
            stage("moba", 0)
            turn(2)
            stage("cross", 2)
            turn(3)

            def down(c, i, per, blocks, first, last):
                pe.wait_ge(lo_done, i * per + (c + 1))
                pe.wait_ge(hid_lo, blocks)
                banks = [[ps[:, 2 * t + nb, :] for nb in range(2)] for t in range(TT)]
                rows_product(hid, range(2), c % NSLOT, 512, banks, first, last,
                             y_half if last else None).then_inc(used, 1)

            def up(c, i, per, bank, norm=None):
                pe.wait_ge(lo_done, i * per + (c + 1))
                transposed_product(hT, c % NSLOT, ps[:, bank, :], norm).then_inc(used, 1)

            def relu_steps(i, opens):
                for j in range(3):
                    c = C_RELU + 1 + 2 * j
                    pe.wait_ge(hraw_done, i * 3 + (j + 1))
                    up(c, i, 6, 4)
                    down(c + 1, i, 6, i * 3 + (j + 1), opens and j == 0, False)

            up(C_RELU, 0, 0, 4, 3)
            relu_steps(0, True)
            with pe.Fori(1, (RELU_BLOCKS - 1) // 3) as i:
                relu_steps(i, False)
            down(C_LAYER - 1, 0, 0, RELU_BLOCKS, False, True)
            turn(4)

            def gated(c0, f, norm):
                b0 = g0 = RELU_BLOCKS + GLU_BLOCKS * f

                def step(i, opens):
                    c = c0 + 2
                    pe.wait_ge(gate_done, i + (g0 + 1))
                    up(c, i, 3, 4)
                    pe.wait_ge(hraw_done, i + (b0 + 1))
                    up(c + 1, i, 3, 5)
                    down(c + 2, i, 3, i + (b0 + 1), opens, False)

                up(c0, 0, 0, 4, norm)
                up(c0 + 1, 0, 0, 5)
                step(0, True)
                with pe.Fori(1, GLU_BLOCKS - 1) as i:
                    step(i, False)
                down(c0 + 3 * GLU_BLOCKS - 1, 0, 0, b0 + GLU_BLOCKS, False, True)

            for layer, kind in enumerate(("diff", "near")):
                f1, c_att, f2 = c_layer(layer)
                gated(f1, 2 * layer, 4 + 3 * layer)
                turn(5 + 3 * layer)
                stage(kind, 5 + 3 * layer)
                turn(6 + 3 * layer)
                gated(f2, 2 * layer + 1, 6 + 3 * layer)
                if layer == 0:
                    turn(7)


_UNUSED = ("gqa_w_in_2", "gqa_w_out_2", "gqa_qk_norm_2")


def kernel(**inputs):
    import concourse.bacc as bacc
    from concourse.bass_utils import run_bass_kernel_spmd

    nc = bacc.Bacc("TRN2", target_bir_lowering=False, num_devices=1)
    arrays, w = {}, {}
    for name, value in inputs.items():
        if name in _UNUSED:
            continue
        arrays[name] = np.ascontiguousarray(value)
        w[name] = nc.dram_tensor(name, arrays[name].shape, mybir.dt.from_np(arrays[name].dtype),
                                 kind="ExternalInput").ap()
    arrays["shape_tables"] = shape_tables()
    table = nc.dram_tensor("shape_tables", arrays["shape_tables"].shape, F32, kind="ExternalInput").ap()
    out = nc.dram_tensor("result", [1, S, D], F32, kind="ExternalOutput").ap()
    build(nc, w, table, out)
    r = run_bass_kernel_spmd(nc, [arrays], core_ids=[0])
    return r.results[0]["result"]
```
